# Optimizing a Trainium2 kernel written in Bass

```python
import jax, jax.numpy as jnp
from jax import lax
import numpy as np

D_MODEL = 1024
BATCH = 1
SEQ = 256
DEPTH = 1
DEC_BATCH = 8
DEC_SEQ = 1
PAST_LEN = 1024
PAGE_SIZE = 128

ATT_HEADS = 8
ATT_HD = D_MODEL // ATT_HEADS
ATT_W = ATT_HEADS * ATT_HD
ROT_DIM = ATT_HD // 4
ROPE_THETA = 500000.0
MOBA_BLOCK = 256
MOBA_TOPK = 3
Q_BLOCK = 64
ML_HEADS = 4
ML_HD = D_MODEL // ML_HEADS
ML_W = ML_HEADS * ML_HD
ML_CHUNK = 64
EPS = 1e-6
SPLIT_SIZES = (ATT_W, ATT_W, ATT_W, ATT_W, ML_W, ML_W, ML_W, ML_W, ML_W, D_MODEL, D_MODEL, ML_HEADS, ML_HEADS)
PROJ_W = 4 * ATT_W + 5 * ML_W + 2 * D_MODEL + 2 * ML_HEADS

kernel_name = 'moba_mlstm_parallel_hybrid_step'

def rms_norm(x, w):
    xf = x.astype(jnp.float32)
    y = xf * lax.rsqrt(jnp.mean(xf * xf, axis=-1, keepdims=True) + EPS)
    return (y * w.astype(jnp.float32)).astype(x.dtype)

def partial_rope(x, pos):
    half = ROT_DIM // 2
    inv = ROPE_THETA ** (-(jnp.arange(half, dtype=jnp.float32) * 2.0) / ROT_DIM)
    ang = pos.astype(jnp.float32)[:, None] * inv[None, :]
    cos, sin = jnp.cos(ang)[:, None, :], jnp.sin(ang)[:, None, :]
    xf = x.astype(jnp.float32)
    x1, x2 = xf[..., :half], xf[..., half:ROT_DIM]
    out = jnp.concatenate([x1 * cos - x2 * sin, x2 * cos + x1 * sin, xf[..., ROT_DIM:]], axis=-1)
    return out.astype(x.dtype)

def branch_inputs(x, pos, norm_w, w_in, b_gates, q_norm_w, k_norm_w):
    B, S, _ = x.shape
    xn = rms_norm(x, norm_w)
    points, acc = [], 0
    for s in SPLIT_SIZES[:-1]:
        acc += s
        points.append(acc)
    aq, ak, av, az, mq, mk, mv, mo, mz, ga, gm, mi, mf = jnp.split(xn @ w_in, points, axis=-1)
    aq = partial_rope(rms_norm(aq.reshape(B, S, ATT_HEADS, ATT_HD), q_norm_w), pos)
    ak = partial_rope(rms_norm(ak.reshape(B, S, ATT_HEADS, ATT_HD), k_norm_w), pos)
    av = av.reshape(B, S, ATT_HEADS, ATT_HD)
    mq = mq.reshape(B, S, ML_HEADS, ML_HD).transpose(0, 2, 1, 3)
    mk = mk.reshape(B, S, ML_HEADS, ML_HD).transpose(0, 2, 1, 3) * (ML_HD ** -0.5)
    mv = mv.reshape(B, S, ML_HEADS, ML_HD).transpose(0, 2, 1, 3)
    gates = jnp.concatenate([mi, mf], axis=-1).astype(jnp.float32) + b_gates.astype(jnp.float32)
    ig = gates[..., :ML_HEADS].transpose(0, 2, 1)
    lf = jax.nn.log_sigmoid(gates[..., ML_HEADS:]).transpose(0, 2, 1)
    return aq, ak, av, az, mq, mk, mv, ig, lf, mo, mz, ga, gm

def moba_prompt(q, k, v):
    B, S, H, hd = q.shape
    nb = -(-S // MOBA_BLOCK)
    pad = ((0, 0), (0, nb * MOBA_BLOCK - S), (0, 0), (0, 0))
    k_blk = jnp.pad(k.astype(jnp.float32), pad).reshape(B, nb, MOBA_BLOCK, H, hd)
    v_blk = jnp.pad(v.astype(jnp.float32), pad).reshape(B, nb, MOBA_BLOCK, H, hd)
    qf = q.astype(jnp.float32)
    k_mean = jnp.mean(k_blk, axis=2)
    gate = jnp.einsum('bshd,bnhd->bhsn', qf, k_mean)
    q_block = jnp.arange(S) // MOBA_BLOCK
    gate = jnp.where(jnp.arange(nb)[None, :] < q_block[:, None], gate, -jnp.inf)
    top = min(MOBA_TOPK, nb)
    _, sel = lax.top_k(gate, top)
    valid = sel < q_block[None, None, :, None]
    k_bh = k_blk.transpose(0, 3, 1, 2, 4)
    v_bh = v_blk.transpose(0, 3, 1, 2, 4)
    nqb = S // Q_BLOCK

    def to_items(t):
        t = jnp.moveaxis(t.reshape(B, H, nqb, Q_BLOCK, *t.shape[3:]), 2, 1)
        return t.reshape(B * nqb, H, Q_BLOCK, *t.shape[4:])

    items = (to_items(qf.transpose(0, 2, 1, 3)), to_items(sel), to_items(valid),
             jnp.repeat(jnp.arange(B, dtype=jnp.int32), nqb), jnp.tile(jnp.arange(nqb, dtype=jnp.int32), B))
    h_ix = jnp.arange(H)[:, None, None]
    k_local = jnp.arange(MOBA_BLOCK)
    q_local = jnp.arange(Q_BLOCK)
    scale = hd ** -0.5
    n_sel = top * MOBA_BLOCK

    def attend(item):
        qi, si, vi, b, qb = item
        kb, vb = k_bh[b], v_bh[b]
        k_sel, v_sel = kb[h_ix, si], vb[h_ix, si]
        s_sel = jnp.einsum('hqd,hqjkd->hqjk', qi, k_sel) * scale
        s_sel = jnp.where(vi[..., None], s_sel, -jnp.inf).reshape(H, Q_BLOCK, n_sel)
        own = (qb * Q_BLOCK) // MOBA_BLOCK
        k_own, v_own = kb[:, own], vb[:, own]
        s_own = jnp.einsum('hqd,hkd->hqk', qi, k_own) * scale
        causal = own * MOBA_BLOCK + k_local[None, :] <= qb * Q_BLOCK + q_local[:, None]
        s_own = jnp.where(causal, s_own, -jnp.inf)
        p = jax.nn.softmax(jnp.concatenate([s_sel, s_own], axis=-1), axis=-1)
        p_sel = p[..., :n_sel].reshape(H, Q_BLOCK, top, MOBA_BLOCK)
        return jnp.einsum('hqjk,hqjkd->qhd', p_sel, v_sel) + jnp.einsum('hqk,hkd->qhd', p[..., n_sel:], v_own)

    out = lax.map(attend, items)
    return out.reshape(B, S, H, hd).astype(q.dtype)

def moba_sample(q, k_new, v_new, cache_k, cache_v, page_table):
    DB, DS, H, hd = q.shape
    n_pages = page_table.shape[1]
    ppb = MOBA_BLOCK // PAGE_SIZE
    n_full = (n_pages * PAGE_SIZE) // MOBA_BLOCK
    own_page0 = n_full * ppb
    scale = hd ** -0.5
    qf = q.astype(jnp.float32)
    parts = []
    if n_full > 0:
        k_full = cache_k[page_table[:, :own_page0]].astype(jnp.float32)
        k_mean = jnp.mean(k_full.reshape(DB, n_full, MOBA_BLOCK, H, hd), axis=2)
        gate = jnp.einsum('bqhd,bnhd->bhqn', qf, k_mean)
        top = min(MOBA_TOPK, n_full)
        _, sel = lax.top_k(gate, top)
        logical = sel[..., None] * ppb + jnp.arange(ppb)
        phys = page_table[jnp.arange(DB)[:, None, None, None, None], logical]
        h_ix = jnp.arange(H)[None, :, None, None, None]
        k_sel = cache_k[phys, :, h_ix, :].reshape(DB, H, DS, top * MOBA_BLOCK, hd)
        v_sel = cache_v[phys, :, h_ix, :].reshape(DB, H, DS, top * MOBA_BLOCK, hd)
        parts.append((jnp.einsum('bqhd,bhqkd->bhqk', qf, k_sel.astype(jnp.float32)) * scale, v_sel, True))
    if n_pages > own_page0:
        k_own = cache_k[page_table[:, own_page0:]].reshape(DB, -1, H, hd)
        v_own = cache_v[page_table[:, own_page0:]].reshape(DB, -1, H, hd)
        parts.append((jnp.einsum('bqhd,bkhd->bhqk', qf, k_own.astype(jnp.float32)) * scale, v_own, False))
    s_new = jnp.einsum('bqhd,bkhd->bhqk', qf, k_new.astype(jnp.float32)) * scale
    s_new = jnp.where(jnp.tril(jnp.ones((DS, DS), dtype=bool)), s_new, -jnp.inf)
    parts.append((s_new, v_new, False))
    p = jax.nn.softmax(jnp.concatenate([s for s, _, _ in parts], axis=-1), axis=-1)
    out = jnp.zeros((DB, DS, H, hd), jnp.float32)
    off = 0
    for s, vals, per_query in parts:
        w = s.shape[-1]
        pb = p[..., off:off + w]
        off += w
        if per_query:
            out = out + jnp.einsum('bhqk,bhqkd->bqhd', pb, vals.astype(jnp.float32))
        else:
            out = out + jnp.einsum('bhqk,bkhd->bqhd', pb, vals.astype(jnp.float32))
    return out.astype(q.dtype)

def mlstm_chunk(carry, chunk):
    c_prev, n_prev, m_prev = (t.astype(jnp.float32) for t in carry)
    q, k, v, ig, lf = (t.astype(jnp.float32) for t in chunk)
    L = q.shape[2]
    b = jnp.cumsum(lf, axis=-1)
    causal = jnp.tril(jnp.ones((L, L), dtype=bool))
    log_w = jnp.where(causal, b[..., :, None] - b[..., None, :] + ig[..., None, :], -jnp.inf)
    log_inter = b + m_prev[..., None]
    m_t = jnp.maximum(log_inter, jnp.max(log_w, axis=-1))
    w_intra = jnp.exp(log_w - m_t[..., None])
    w_inter = jnp.exp(log_inter - m_t)
    s = jnp.einsum('bhtd,bhsd->bhts', q, k) * w_intra
    num = w_inter[..., None] * jnp.einsum('bhtd,bhde->bhte', q, c_prev) + jnp.einsum('bhts,bhse->bhte', s, v)
    den = w_inter * jnp.einsum('bhtd,bhd->bht', q, n_prev) + jnp.sum(s, axis=-1)
    h = num / jnp.maximum(jnp.abs(den), jnp.exp(-m_t))[..., None]
    m_new = m_t[..., -1]
    a_prev = jnp.exp(b[..., -1] + m_prev - m_new)
    a_s = jnp.exp(b[..., -1:] - b + ig - m_new[..., None])
    c_new = a_prev[..., None, None] * c_prev + jnp.einsum('bhs,bhsd,bhse->bhde', a_s, k, v)
    n_new = a_prev[..., None] * n_prev + jnp.einsum('bhs,bhsd->bhd', a_s, k)
    return (c_new, n_new, m_new), h

def mlstm_prompt(q, k, v, ig, lf):
    B, H, S, dk = q.shape
    dv = v.shape[-1]
    nc = S // ML_CHUNK

    def chunks(t):
        return jnp.moveaxis(t.reshape(B, H, nc, ML_CHUNK, *t.shape[3:]), 2, 0)

    init = (jnp.zeros((B, H, dk, dv), jnp.float32), jnp.zeros((B, H, dk), jnp.float32), jnp.zeros((B, H), jnp.float32))
    state, h = lax.scan(mlstm_chunk, init, (chunks(q), chunks(k), chunks(v), chunks(ig), chunks(lf)))
    h = jnp.moveaxis(h, 0, 2).reshape(B, H, S, dv).transpose(0, 2, 1, 3)
    return h, state

def merge_branches(x, attn, az, h, mo, mz, ga, gm, mh_norm_w, w_proj_attn, w_proj_mlstm, w_out):
    B, S, _ = x.shape
    h = h.astype(x.dtype).reshape(B, S, ML_W) * jax.nn.sigmoid(mo)
    h = rms_norm(h.reshape(B, S, ML_HEADS, ML_HD), mh_norm_w).reshape(B, S, ML_W)
    y_att = (attn.reshape(B, S, ATT_W) * jax.nn.silu(az)) @ w_proj_attn
    y_ml = (h * jax.nn.silu(mz)) @ w_proj_mlstm
    return x + (jax.nn.sigmoid(ga) * y_att + jax.nn.sigmoid(gm) * y_ml) @ w_out

def setup_inputs(seed: int = 0) -> dict:
    key = jax.random.key(seed)
    ks = jax.random.split(key, 20)
    n_pages = PAST_LEN // PAGE_SIZE
    n_used = DEC_BATCH * n_pages
    n_pool = (n_used * 5) // 4
    nrm = jax.random.normal
    page_table = jax.random.permutation(ks[0], n_pool)[:n_used].reshape(DEC_BATCH, n_pages).astype(jnp.int32)
    b_gates = jnp.concatenate([0.1 * nrm(ks[1], (DEPTH, ML_HEADS)), 3.0 + 0.5 * nrm(ks[2], (DEPTH, ML_HEADS))], axis=-1)
    return {
        'x_prompt': nrm(ks[3], (BATCH, SEQ, D_MODEL), jnp.float32),
        'x_sample': nrm(ks[4], (DEC_BATCH, DEC_SEQ, D_MODEL), jnp.float32),
        'cache_k': nrm(ks[5], (DEPTH, n_pool, PAGE_SIZE, ATT_HEADS, ATT_HD), jnp.float32),
        'cache_v': nrm(ks[6], (DEPTH, n_pool, PAGE_SIZE, ATT_HEADS, ATT_HD), jnp.float32),
        'page_table': page_table,
        'state_mlstm_C': 0.05 * nrm(ks[7], (DEPTH, DEC_BATCH, ML_HEADS, ML_HD, ML_HD), jnp.float32),
        'state_mlstm_n': 0.1 * nrm(ks[8], (DEPTH, DEC_BATCH, ML_HEADS, ML_HD), jnp.float32),
        'state_mlstm_m': 0.5 * nrm(ks[9], (DEPTH, DEC_BATCH, ML_HEADS), jnp.float32),
        'norm_w': 1.0 + 0.02 * nrm(ks[10], (DEPTH, D_MODEL), jnp.float32),
        'w_in': nrm(ks[11], (DEPTH, D_MODEL, PROJ_W), jnp.float32) * D_MODEL ** -0.5,
        'b_gates': b_gates,
        'q_norm_w': 1.0 + 0.02 * nrm(ks[12], (DEPTH, ATT_HD), jnp.float32),
        'k_norm_w': 1.0 + 0.02 * nrm(ks[13], (DEPTH, ATT_HD), jnp.float32),
        'mh_norm_w': 1.0 + 0.02 * nrm(ks[14], (DEPTH, ML_HD), jnp.float32),
        'w_proj_attn': nrm(ks[15], (DEPTH, ATT_W, D_MODEL), jnp.float32) * ATT_W ** -0.5,
        'w_proj_mlstm': nrm(ks[16], (DEPTH, ML_W, D_MODEL), jnp.float32) * ML_W ** -0.5,
        'w_out': nrm(ks[17], (DEPTH, D_MODEL, D_MODEL), jnp.float32) * D_MODEL ** -0.5,
    }

def reference(x_prompt, x_sample, cache_k, cache_v, page_table, state_mlstm_C, state_mlstm_n, state_mlstm_m,
              norm_w, w_in, b_gates, q_norm_w, k_norm_w, mh_norm_w, w_proj_attn, w_proj_mlstm, w_out):
    S = x_prompt.shape[1]
    DS = x_sample.shape[1]
    past = page_table.shape[1] * PAGE_SIZE
    pos_p = jnp.arange(S, dtype=jnp.int32)
    pos_s = past + jnp.arange(DS, dtype=jnp.int32)
    st_dtype = state_mlstm_C.dtype
    y_p, y_s = x_prompt, x_sample
    k_p, v_p, c_p, n_p, m_p = [], [], [], [], []
    k_s, v_s, c_s, n_s, m_s = [], [], [], [], []
    for l in range(DEPTH):
        aq, ak, av, az, mq, mk, mv, ig, lf, mo, mz, ga, gm = branch_inputs(
            y_p, pos_p, norm_w[l], w_in[l], b_gates[l], q_norm_w[l], k_norm_w[l])
        attn = moba_prompt(aq, ak, av)
        h, (c_new, n_new, m_new) = mlstm_prompt(mq, mk, mv, ig, lf)
        y_p = merge_branches(y_p, attn, az, h, mo, mz, ga, gm, mh_norm_w[l], w_proj_attn[l], w_proj_mlstm[l], w_out[l])
        k_p.append(ak); v_p.append(av); c_p.append(c_new); n_p.append(n_new); m_p.append(m_new)
        aq, ak, av, az, mq, mk, mv, ig, lf, mo, mz, ga, gm = branch_inputs(
            y_s, pos_s, norm_w[l], w_in[l], b_gates[l], q_norm_w[l], k_norm_w[l])
        attn = moba_sample(aq, ak, av, cache_k[l], cache_v[l], page_table)
        (c_new, n_new, m_new), h = mlstm_chunk((state_mlstm_C[l], state_mlstm_n[l], state_mlstm_m[l]), (mq, mk, mv, ig, lf))
        h = h.transpose(0, 2, 1, 3)
        y_s = merge_branches(y_s, attn, az, h, mo, mz, ga, gm, mh_norm_w[l], w_proj_attn[l], w_proj_mlstm[l], w_out[l])
        k_s.append(ak); v_s.append(av); c_s.append(c_new); n_s.append(n_new); m_s.append(m_new)
    return (y_p, y_s,
            jnp.stack(k_p), jnp.stack(v_p), jnp.stack(c_p).astype(st_dtype), jnp.stack(n_p).astype(st_dtype), jnp.stack(m_p).astype(st_dtype),
            jnp.stack(k_s), jnp.stack(v_s), jnp.stack(c_s).astype(st_dtype), jnp.stack(n_s).astype(st_dtype), jnp.stack(m_s).astype(st_dtype))


_drawn_inputs = setup_inputs


def setup_inputs(seed=0):
    import zlib

    import numpy as np

    out = dict(_drawn_inputs(seed))
    spreads = {}
    factors = {'cache_k': 3.907,
     'cache_v': 3.163,
     'q_norm_w': 8.0,
     'k_norm_w': 7.568,
     'mh_norm_w': 23.896}
    for name, (base, spread) in spreads.items():
        noise = np.random.default_rng([zlib.crc32(name.encode()), seed]).standard_normal(out[name].shape)
        drawn = base * np.exp(spread * noise) if base else spread * noise
        out[name] = __import__('jax').numpy.asarray(drawn.astype(out[name].dtype))
    for name, factor in factors.items():
        out[name] = (out[name] * factor).astype(out[name].dtype)
    return out
```

```python
from contextlib import ExitStack

import numpy as np

import concourse.bass as bass
from concourse import mybir

F32 = mybir.dt.float32
F32R = mybir.dt.float32r
I32 = mybir.dt.int32
ALU = mybir.AluOpType
ACT = mybir.ActivationFunctionType
AX = mybir.AxisListType
ds = bass.ds

P = 128
D = 1024
SEQ = 256
NB = 8
T = SEQ + NB
KC = D // P
HEADS = 8
HD = 128
MH = 4
MHD = 256
EC = MHD // P
PAST = 1024
PAGE = 128
PAGES = PAST // PAGE
BLOCK = 256
PPB = BLOCK // PAGE
NBLK = PAST // BLOCK
TOPK = 3
ROT = HD // 4
THETA = 500000.0
EPS = 1e-6
SCALE = HD ** -0.5
BIG = 1e30

AQ, AK, AV, AZ, MQ, MK, MV, MO, MZ, GA, GM, GATES = (D * i for i in range(12))
GROUPS = [AK, MQ, MK, MV, AV, AZ, MO, MZ]
CHUNKS = 2 * len(GROUPS)
WRAW = 2
WSPLIT = 4
AHEAD = 3
LO = 32
KSLOTS = 4
VSLOTS = 4
CSLOTS = 4
JOBS = 4

C_ID, C_ONE, C_ROT, C_MASK, C_TRIT, C_COS, C_SIN, C_DEL, C_RANK, C_EPS, C_END = (
    0, 128, 256, 384, 768, 896, 896 + T, 896 + 2 * T, 896 + 2 * T + 64, 896 + 2 * T + 96, 896 + 2 * T + 97)

DVE_STEPS = 76
ACT_STEPS = 3


def at(j, per, k, base=0):
    return j * per + (base + k)


class Chain:

    def __init__(self, eng, sem):
        self.eng, self.sem, self.base, self.n = eng, sem, 0, 0

    def link(self, ins):
        self.n += 1
        ins.then_inc(self.sem, 1)
        self.eng.wait_ge(self.sem, self.base + self.n)

    def step(self, ins):
        self.n += 1
        ins.then_inc(self.sem, 1)


def build(nc, a, o):
    ctx = ExitStack()
    with ctx:
        def sb(name, shape, dt=F32):
            return ctx.enter_context(nc.sbuf_tensor(name, shape, dt))

        def sem(name):
            return ctx.enter_context(nc.semaphore(name))

        cst = sb("cst", [P, C_END])
        cols = sb("cols", [P, KC + 2 + EC])
        bg = sb("bg", [MH, 2])
        wraw = sb("wraw", [P, WRAW, KC, 256])
        w2 = sb("w2", [P, WSPLIT, 2, KC, P], F32R)
        xn2 = sb("xn2", [P, 2, KC, T], F32R)
        kpages = sb("kpages", [P, KSLOTS, D])
        vpages = sb("vpages", [P, VSLOTS, D])
        qT = sb("qT", [P, HEADS, T])
        mlg = sb("mlg", [P, KC, T])
        qs2 = sb("qs2", [LO + NB, D], F32R)
        rows2 = sb("rows2", [LO + NB, 2 * SEQ], F32R)
        mvs2 = sb("mvs2", [LO + NB, MHD], F32R)
        eye2 = sb("eye2", [LO + NB, NB], F32R)
        nnat = sb("nnat", [NB, D])
        ptab = sb("ptab", [1, NB * PAGES], I32)
        qbc = sb("qbc", [P, 2, D])
        cslot = sb("cslot", [P, CSLOTS, EC, MHD])
        qTc = sb("qTc", [P, 2, T])
        kT = sb("kT", [P, 2, T])
        sq = sb("sq", [P, 2, T])
        rs = sb("rs", [P, 2, T])
        mqT = sb("mqT", [P, 2, T])
        mkT = sb("mkT", [P, 2, T])
        vT = sb("vT", [P, 2, T])
        zraw = sb("zraw", [P, 3, 2, T])
        zsig = sb("zsig", [P, 2, 2, T])
        k_nat = sb("k_nat", [P, 2, 256])
        v_nat = sb("v_nat", [P, 2, 256])
        mk_nat = sb("mk_nat", [P, 2, 256])
        mv_nat = sb("mv_nat", [P, 2, 256])
        mks = sb("mks", [NB, MHD])
        mvs = sb("mvs", [NB, MHD])
        att = sb("att", [P, 2, 384])
        pT = sb("pT", [P, 2, 384])
        hT = sb("hT", [P, 2, T])
        va = sb("va", [P, 2, 256])
        nnew = sb("nnew", [1, MHD])
        sco = sb("sco", [P, 2, PAGES, HEADS])
        prob = sb("prob", [P, 2, PAGES, HEADS])
        att2 = sb("att2", [P, 2, KC, T], F32R)
        gsm = sb("gsm", [P, 2, 4, 32])
        mx = sb("mx", [P, 2, HEADS])
        gm = sb("gm", [P, 2, HEADS])
        gmax = sb("gmax", [P, NB, HEADS])
        lsum = sb("lsum", [P, NB, HEADS])
        accS = sb("accS", [P, NB + 1, HEADS])
        accr = sb("accr", [HEADS, HD])
        kTs = sb("kTs", [P, HEADS, NB])
        vTs = sb("vTs", [P, HEADS, NB])
        qTs = sb("qTs", [P, HEADS, NB])
        selc = sb("selc", [LO + NB, 3], F32R)
        rows = sb("rows", [MH, 2, SEQ])
        uT = sb("uT", [P, 2, MH])
        gN = sb("gN", [NB, 6, MH])
        wN = sb("wN", [NB, 3, MH])
        mstate = sb("mstate", [NB, MH])
        msnew = sb("msnew", [NB, MH])
        gexp = sb("gexp", [NB, 3 * MH, NB])
        bcg = sb("bcg", [P, 3, MH, NB])
        nT = sb("nT", [P, MH, EC, NB])
        qmask = sb("qmask", [P, EC, NB, NB])
        qprod = sb("qprod", [P, 2, EC, NB])
        kc = sb("kc", [P, EC, NB])
        w3 = sb("w3", [NB, 3])
        sm1 = sb("sm1", [NB, 8])
        hs = sb("hs", [NB, MHD])
        ssx = sb("ssx", [P, 3, 4])
        nm = sb("nm", [P, 2, 2])
        rsum = sb("rsum", [P, 2, 2])

        pj = [ctx.enter_context(nc.psum_tensor(f"pj{i}", [P, 512], F32)) for i in range(2)]
        wk = [ctx.enter_context(nc.psum_tensor(f"wk{i}", [P, 512], F32)) for i in range(4)]
        pa = [ctx.enter_context(nc.psum_tensor(f"pa{i}", [P, 512], F32)) for i in range(2)]

        ident = cst[:, C_ID:C_ID + P]
        ones = cst[:, C_ONE:C_ONE + P]
        rot = cst[:, C_ROT:C_ROT + P]
        mask3 = cst[:, C_MASK:C_MASK + 384]
        triT = cst[:, C_TRIT:C_TRIT + P]
        cos = cst[:, C_COS:C_COS + T]
        sin = cst[:, C_SIN:C_SIN + T]
        delta = cst[:, C_DEL:C_DEL + 64].rearrange("p (b c) -> p b c", b=NB)
        rank0 = cst[:, C_RANK:C_RANK + 32].rearrange("p (n h) -> p n h", n=NBLK)
        normw, qkw, mhw = cols[:, 0:KC], cols[:, KC:KC + 2], cols[:, KC + 2:KC + 2 + EC]
        epsc = cst[:, C_EPS:C_EPS + 1]
        rawT = sq
        wt, sw = att[:, 0, :], att[:, 1, :]
        emt, dn = pT[:, 0, 0:SEQ], pT[:, 1, 0:SEQ]
        cnew = va
        ctmp = zsig[:, :, :, :].rearrange("p a c t -> p (a c t)")[:, 0:2 * EC * MHD].rearrange("p (b c e) -> p b c e", b=2, c=EC)
        nso = vT[0:NB, 0, 0:MHD]
        accd = qbc[0:HEADS, 0, :].rearrange("p (h d) -> p h d", h=HEADS)
        xin = vpages[:, 0:3, :]
        wg = kpages[:, 3, 0:64].rearrange("p (k g) -> p k g", k=KC)
        gr = zraw[0:MH].rearrange("p a c t -> p (a c) t")
        xnT = mlg
        epi = zraw[:, 0, :, :].rearrange("p c t -> p (c t)")[:, 0:512].rearrange("p (i n) -> p i n", i=8)
        sga, sgm = (x[:, :, :].rearrange("p s d -> p (s d)")[:, 0:KC * T].rearrange("p (k t) -> p k t", k=KC) for x in (kpages, vpages))
        mrg2, mlg2 = att2, xn2
        yT = hT
        yout = kpages[:, 0:3, :]
        xres = [qbc[:, 0, :], qbc[:, 1, :], nnat[:, :]]

        boot, boot_x = sem("boot"), sem("boot_x")
        wload = [sem(f"wload{i}") for i in range(WRAW)]
        whi_ready, wlo_ready = sem("whi_ready"), sem("wlo_ready")
        kload = [sem(f"kload{i}") for i in range(KSLOTS)]
        vload = [sem(f"vload{i}") for i in range(VSLOTS)]
        cload = [sem(f"cload{i}") for i in range(CSLOTS)]
        cstore = [sem(f"cstore{i}") for i in range(CSLOTS)]
        k_used, v_used = sem("k_used"), sem("v_used")
        dve_step, act_step = sem("dve_step"), sem("act_step")
        xt_ps, xt_even, xt_odd, gate_ps, gate_raw, gate_e, gate_ln = (
            sem("xt_ps"), sem("xt_even"), sem("xt_odd"), sem("gate_ps"), sem("gate_raw"), sem("gate_e"), sem("gate_ln"))
        rows_ready, gtr_ps, wN_in, wN_ready, gexp_ready, bcg_ps = (
            sem("rows_ready"), sem("gtr_ps"), sem("wN_in"), sem("wN_ready"), sem("gexp_ready"), sem("bcg_ps"))
        x_scaled, xss, nt_ps, qs_ps, q_ready, boot_done = (
            sem("x_scaled"), sem("xss"), sem("nt_ps"), sem("qs_ps"), sem("q_ready"), sem("boot_done"))
        xhi_ready, xlo_ready = sem("xhi_ready"), sem("xlo_ready")
        proj, norm_ps, qbc_ps, ktr_ps, mktr_ps, st_ps, bc_ps, mvtr_ps, g_ps, avtr_ps, den_ps, num_ps = (
            sem(n) for n in "proj norm_ps qbc_ps ktr_ps mktr_ps st_ps bc_ps mvtr_ps g_ps avtr_ps den_ps num_ps".split())
        qc_ps, vbc_ps, cn_ps, l_ps, sc_ps, acct_ps, ptr_ps, pvh_ps, hst_ps, mln_ps = (
            sem(n) for n in "qc_ps vbc_ps cn_ps l_ps sc_ps acct_ps ptr_ps pvh_ps hst_ps mln_ps".split())
        evac, qbc_ready, rs_ready, w_ready, ctmp_ready, prob_ready, cn_ready, att_exp, sig_ready, pT_ready, sqh_ready, mrs_ready = (
            sem(n) for n in "evac qbc_ready rs_ready w_ready ctmp_ready prob_ready cn_ready att_exp sig_ready pT_ready sqh_ready mrs_ready".split())
        selc_ready, kT_ready, knat_ready, mk_ready, wl_ready, mv_ready, qm_ready, sw_ready, vnat_ready, g_read, mx_ready = (
            sem(n) for n in "selc_ready kT_ready knat_ready mk_ready wl_ready mv_ready qm_ready sw_ready vnat_ready g_read mx_ready".split())
        va_ready, h_ready, pm_ready, c_ready, l_read, accr_ready, smax_ready, acc_ready, p_ready, qc_read, hs_ready, attg_ready, hmo_ready, mlg_ready, nso_ready, silu_ready = (
            sem(n) for n in "va_ready h_ready pm_ready c_ready l_read accr_ready smax_ready acc_ready p_ready qc_read hs_ready attg_ready hmo_ready mlg_ready nso_ready silu_ready".split())
        mvlo_ready = sem("mvlo_ready")
        table_load, gmax_ready = sem("table_load"), sem("gmax_ready")
        st_k, st_v, st_c, st_n, st_ns, st_misc, st_y = (sem(n) for n in "st_k st_v st_c st_n st_ns st_misc st_y".split())
        ep_ps, ep_act, ep_dve, ep_y, xres_load, ywk = sem("ep_ps"), sem("ep_act"), sem("ep_dve"), sem("ep_y"), sem("xres_load"), sem("ywk")
        sg_ready, a2_hi, a2_lo, mrg_hi, mrg_lo, yT_ready, y_ps = (
            sem("sg_ready"), sem("a2_hi"), sem("a2_lo"), sem("mrg_hi"), sem("mrg_lo"), sem("yT_ready"), sem("y_ps"))

        w_in = a["w_in"][0].rearrange("(k p) n -> p k n", p=P)
        block = ctx.enter_context(nc.Block())

        @block.sync
        def _(sp):
            for t in range(2):
                sp.dma_start(xin[:, t, :], a["x_prompt"][0, t * P:(t + 1) * P, :]).then_inc(boot_x, 16)
            sp.dma_start(xin[0:NB, 2, :], a["x_sample"][:, 0, :]).then_inc(boot_x, 16)
            sp.dma_start(cst[:, :], a["consts"]).then_inc(boot, 16)
            sp.dma_start(cols[:, :], a["columns"]).then_inc(boot, 16)
            sp.dma_start(bg[:, :], a["gate_bias"]).then_inc(boot, 16)
            sp.dma_start(kpages[:, 3, 0:64], a["gate_weights"]).then_inc(boot, 16)
            sp.dma_start(nnat[:, :], a["state_mlstm_n"][0].rearrange("b h d -> b (h d)")).then_inc(boot, 16)
            sp.dma_start(mstate[:, :], a["state_mlstm_m"][0]).then_inc(boot, 16)

            def load_w(n, src, used=None):
                if used is not None:
                    sp.wait_ge(wlo_ready, used)
                sp.dma_start(wraw[:, n % WRAW], src).then_inc(wload[n % WRAW], 16)

            for n in range(4):
                load_w(n, w_in[:, :, AQ + 256 * n:AQ + 256 * (n + 1)], 2 * n - 2 if n >= WRAW else None)
            with sp.Fori(0, JOBS) as j:
                for n, g in enumerate(GROUPS):
                    load_w(4 + n, w_in[:, :, ds(j * 256 + g, 256)], at(j, CHUNKS, 2 * n - 2, HEADS))
            late = [w_in[:, :, GA:GA + D], w_in[:, :, GM:GM + D]]
            late += [a[name][0].rearrange("(k p) n -> p k n", p=P) for name in ("w_proj_attn", "w_proj_mlstm", "w_out")]
            for m, view in enumerate(late):
                for q in range(4):
                    load_w(4 * m + q, view[:, :, q * 256:(q + 1) * 256], at(JOBS, CHUNKS, 2 * (4 * m + q) - 2, HEADS))
                if m == 2:
                    sp.wait_ge(acc_ready, 2 * JOBS + 1)
                    sp.wait_ge(nso_ready, JOBS)
                    for t in range(2):
                        sp.dma_start(xres[t], a["x_prompt"][0, t * P:(t + 1) * P, :]).then_inc(xres_load, 16)
                    sp.dma_start(xres[2], a["x_sample"][:, 0, :]).then_inc(xres_load, 16)
            for half in range(2):
                sp.wait_ge(ep_y, 4 * (half + 1))
                cut = slice(half * 512, (half + 1) * 512)
                for t in range(2):
                    sp.dma_start(o["y_p"][0, t * P:(t + 1) * P, cut], yout[:, t, cut]).then_inc(st_y, 16)
                sp.dma_start(o["y_s"][:, 0, cut], yout[0:NB, 2, cut]).then_inc(st_y, 16)
            sp.wait_ge(st_y, 96)
            sp.wait_ge(st_k, 16 * (JOBS + 1))
            sp.wait_ge(st_v, 16 * (JOBS + 1))
            sp.wait_ge(st_c, 16 * (JOBS + 1))
            sp.wait_ge(st_n, 16 * (JOBS + 1))
            sp.wait_ge(st_ns, 16 * (JOBS + 1))
            sp.wait_ge(st_misc, 16 * 4)
            for s in cstore:
                sp.wait_ge(s, 16 * (2 * JOBS + 1))

        @block.gpsimd
        def _(pool):
            pool.dma_start(ptab[:, :], a["page_table"].rearrange("(o b) n -> o (b n)", o=1)).then_inc(table_load, 16)
            pool.wait_ge(table_load, 16)

            def page(cache, tile, b, pg, used):
                phys = pool.value_load(ptab[0:1, ds(b * PAGES + pg, 1)], min_val=0, max_val=cache.shape[1] - 1)
                pool.wait_ge(used, at(b, PAGES, pg + 1))
                src = cache[0, ds(phys, 1)].rearrange("o t h d -> t (o h d)")
                return pool.dma_start(tile, src)

            def keys(b, pages):
                for pg in pages:
                    page(a["cache_k"], kpages[:, pg % KSLOTS, :], b, pg, k_used).then_inc(kload[pg % KSLOTS], 16)

            def values(b, pages):
                for pg in pages:
                    page(a["cache_v"], vpages[:, pg % VSLOTS, :], b, pg, v_used).then_inc(vload[pg % VSLOTS], 16)

            def all_max(j, odd):
                count = at(j, 2, odd + 1)
                pool.wait_ge(table_load, 16)
                pool.wait_ge(mx_ready, count)
                nc.gpsimd.partition_all_reduce(gm[:, odd, :], mx[:, odd, :], P, bass.bass_isa.ReduceOp.max).then_inc(gmax_ready, 1)

            first, second = range(PAGES // 2), range(PAGES // 2, PAGES)
            keys(0, first)
            values(0, first)

            def step(j, last):
                b = j * 2
                keys(b, second)
                keys(b + 1, first)
                all_max(j, 0)
                keys(b + 1, second)
                values(b, second)
                if not last:
                    keys(b + 2, first)
                all_max(j, 1)
                values(b + 1, first)
                values(b + 1, second)
                if not last:
                    values(b + 2, first)

            with pool.Fori(0, JOBS - 1) as j:
                step(j, False)
            step(JOBS - 1, True)

        @block.tensor
        def _(pe):
            mm = nc.tensor.matmul

            def tr(out, in_, rows_):
                return nc.tensor.transpose(out, in_, ident[0:rows_, 0:rows_])

            def columns_of(out, in_, eye):
                return mm(out, in_, eye, start=True, stop=True)

            pe.wait_ge(boot, 96)

            for k in range(KC):
                if k == 0:
                    pe.wait_ge(x_scaled, 3)
                if k >= 4:
                    pe.wait_ge((xt_even, xt_odd)[k % 2], (k - 4) // 2 + 1)
                for t in range(2):
                    tr(wk[k % 4][:, t * P:(t + 1) * P], xin[:, t, k * P:(k + 1) * P], P)
                tr(wk[k % 4][:, SEQ:T], xin[0:NB, 2, k * P:(k + 1) * P], NB).then_inc(xt_ps, 1)
            pe.wait_ge(xt_even, KC // 2)
            pe.wait_ge(xt_odd, KC // 2)

            for g in range(2):
                for k in range(KC):
                    last = mm(wk[g][0:MH, 0:T], wg[:, k, g * MH:(g + 1) * MH], xnT[:, k, :], start=(k == 0), stop=(k == KC - 1))
                last.then_inc(gate_ps, 1)
            for i in range(MH * EC):
                last = tr(wk[2][:, i * NB:(i + 1) * NB], nnat[:, i * P:(i + 1) * P], NB)
            last.then_inc(nt_ps, 1)

            def project(bank, q, src, n, parts=None):
                pe.wait_ge(whi_ready, n)
                for k in range(KC):
                    if parts:
                        pe.wait_ge(parts, k + 1)
                    for g in range(2):
                        mm(bank[:, 0:T], w2[:, q, 0, k, :], src[:, g, k, :], start=(k == 0 and g == 0), stop=False)
                pe.wait_ge(wlo_ready, n)
                for k in range(KC):
                    last = mm(bank[:, 0:T], w2[:, q, 1, k, :], src[:, 0, k, :], start=False, stop=(k == KC - 1))
                last.then_inc(proj, 1)

            def norm_sums(ss, ro, i, src):
                mm(ss[:, 0:T], ones, sq[:, i, :], start=True, stop=True)
                mm(ro[:, 0:T], rot, src, start=True, stop=True).then_inc(norm_ps, 1)

            for h in range(HEADS + 1):
                if h < HEADS:
                    if h == 0:
                        pe.wait_ge(xlo_ready, KC)
                    if h >= 2:
                        pe.wait_ge(evac, h - 1)
                    project(pj[h % 2], h % WSPLIT, xn2, h + 1)
                if h == 4:
                    pe.wait_ge(rows_ready, 1)
                    for t in range(2):
                        tr(pa[0][:, t * MH:(t + 1) * MH], gr[:, 2, t * P:(t + 1) * P], MH)
                    tr(pa[1][0:NB, 0:MH], gr[:, 0, SEQ:T], MH)
                    tr(pa[1][0:NB, MH:2 * MH], gr[:, 1, SEQ:T], MH).then_inc(gtr_ps, 1)
                if h >= 1:
                    g = h - 1
                    pe.wait_ge(evac, g + 1)
                    if g == 0:
                        pe.wait_ge(gate_raw, 2)
                        pe.wait_ge(bcg_ps, 1)
                    if g >= 2:
                        pe.wait_ge(q_ready, g - 1)
                    norm_sums(wk[2 * (g % 2)], wk[2 * (g % 2) + 1], g % 2, qT[:, g, :])

            pe.wait_ge(q_ready, HEADS)
            for h in range(HEADS):
                last = tr(wk[2 + h // 4][0:NB, (h % 4) * P:(h % 4 + 1) * P], qT[:, h, SEQ:T], P)
            last.then_inc(qs_ps, 1)
            pe.wait_ge(gexp_ready, 1)
            mm(pa[0][:, 64:64 + 96], ones[0:NB, 0:P], gexp[:, :, :].rearrange("p a b -> p (a b)"), start=True, stop=True)\
                .then_inc(bcg_ps, 1)

            def sample_columns(bank):
                columns_of(bank[:, 0:HEADS], accr[:, :], ident[0:HEADS, 0:HEADS]).then_inc(acct_ps, 1)

            with pe.Fori(0, JOBS) as j:
                def chunk(c):
                    pe.wait_ge(evac, at(j, CHUNKS, c - 1, HEADS))
                    project(pj[c % 2], c % WSPLIT, xn2, at(j, CHUNKS, c + 1, HEADS))

                chunk(0)
                pe.wait_ge(accr_ready, at(j, 2, 1))
                pe.wait_ge(mrs_ready, at(j, 1, 1))
                pe.wait_ge(selc_ready, at(j, 1, 1))
                for odd in range(2):
                    for half in range(2):
                        mm(wk[2 * odd + half][:, :], selc[:, odd:odd + 1].broadcast_to([LO + NB, P]), qs2[:, half * 512:(half + 1) * 512],
                           start=True, stop=True).then_inc(qbc_ps, 1)
                def block_sums(odd, bank):
                    pe.wait_ge(k_used, at(j, 16, 8 * odd + 8, KSLOTS))
                    mm(bank[:, 0:64], ones, sco[:, odd].rearrange("p a h -> p (a h)"), start=True, stop=True).then_inc(g_ps, 1)

                def query_states(bs):
                    for b in bs:
                        pe.wait_ge(cload[b % CSLOTS], at(j, 32, 16 * (b // CSLOTS + 1)))
                        for d in range(EC):
                            last = mm(wk[2][0:NB, 0:MHD], qmask[:, d, b, :], cslot[:, b % CSLOTS, d, :],
                                      start=(b == 0 and d == 0), stop=(b == NB - 1 and d == EC - 1), skip_group_check=True)
                    last.then_inc(qc_ps, 1)

                def value_rows(pair, bank):
                    for i in range(2):
                        last = mm(bank[:, i * MHD:(i + 1) * MHD], eye2[:, 2 * pair + i:2 * pair + i + 1].broadcast_to([LO + NB, P]), mvs2[:, :], start=True, stop=True)
                    last.then_inc(vbc_ps, 1)

                def prob_sums(odd, bank):
                    pe.wait_ge(prob_ready, at(j, 2, odd + 1))
                    mm(bank[:, 0:64], ones, prob[:, odd].rearrange("p a h -> p (a h)"), start=True, stop=True).then_inc(l_ps, 1)

                def cached_values(odd, pages):
                    pe.wait_ge(accr_ready, at(j, 2, odd + 1))
                    for pg in pages:
                        pe.wait_ge(vload[pg % VSLOTS], at(j, 64, 16 * (2 * odd + pg // VSLOTS + 1)))
                        for half in range(2):
                            last = mm(pa[half][0:HEADS, :], prob[:, odd, pg, :], vpages[:, pg % VSLOTS, half * 512:(half + 1) * 512],
                                      start=(pg == 0), stop=(pg == PAGES - 1))
                        last.then_inc(v_used, 1)

                def prompt_scores(i):
                    bank = wk[1 + 2 * i]
                    mm(bank[:, 0:P], qTc[:, i, 0:P], kT[:, i, 0:P], start=True, stop=True)
                    mm(bank[:, P:384], qTc[:, i, P:SEQ], kT[:, i, 0:SEQ], start=True, stop=True).then_inc(sc_ps, 1)

                chunk(1)
                chunk(2)
                sample_columns(pa[0])
                for i in range(2):
                    pe.wait_ge(evac, at(j, CHUNKS, i + 1, HEADS))
                    pe.wait_ge(qbc_ready, at(j, 4, 2 * i + 2))
                    norm_sums(wk[2 * i], wk[2 * i + 1], i, kT[:, i, :])
                chunk(3)
                chunk(4)
                chunk(5)
                pe.wait_ge(kT_ready, at(j, 2, 2))
                for t in range(2):
                    for i in range(2):
                        last = tr(wk[0][:, t * 256 + i * P:t * 256 + (i + 1) * P], kT[:, i, t * P:(t + 1) * P], P)
                last.then_inc(ktr_ps, 1)
                chunk(6)
                pe.wait_ge(evac, at(j, CHUNKS, 6, HEADS))
                for t in range(2):
                    for i in range(2):
                        last = tr(wk[1][:, t * 256 + i * P:t * 256 + (i + 1) * P], mkT[:, i, t * P:(t + 1) * P], P)
                last.then_inc(mktr_ps, 1)
                for i in range(2):
                    last = tr(wk[2][0:NB, i * P:(i + 1) * P], mkT[:, i, SEQ:T], P)
                last.then_inc(mktr_ps, 1)
                pe.wait_ge(knat_ready, at(j, 1, 1))
                mm(wk[0][:, :], selc[:, 2:3].broadcast_to([LO + NB, P]), rows2[:, :], start=True, stop=True).then_inc(bc_ps, 1)
                pe.wait_ge(acc_ready, at(j, 2, 1))
                block_sums(0, pa[0])
                chunk(7)
                chunk(8)
                pe.wait_ge(evac, at(j, CHUNKS, 8, HEADS))
                pe.wait_ge(mk_ready, at(j, 2, 2))
                for t in range(2):
                    for i in range(2):
                        last = tr(wk[1][:, t * 256 + i * P:t * 256 + (i + 1) * P], rawT[:, i, t * P:(t + 1) * P], P)
                last.then_inc(mvtr_ps, 1)
                for i in range(2):
                    last = tr(wk[2][0:NB, i * P:(i + 1) * P], rawT[:, i, SEQ:T], P)
                last.then_inc(mvtr_ps, 1)
                for i in range(2):
                    mm(wk[3][:, 0:SEQ], mkT[:, i, 0:P], mqT[:, i, 0:SEQ], start=(i == 0), stop=(i == 1))
                for i in range(2):
                    last = mm(wk[3][:, SEQ:384], mkT[:, i, P:SEQ], mqT[:, i, P:SEQ], start=(i == 0), stop=(i == 1))
                last.then_inc(st_ps, 1)
                chunk(9)
                chunk(10)
                pe.wait_ge(evac, at(j, CHUNKS, 10, HEADS))
                pe.wait_ge(mv_ready, at(j, 2, 2))
                for t in range(2):
                    for i in range(2):
                        last = tr(wk[2][:, t * 256 + i * P:t * 256 + (i + 1) * P], vT[:, i, t * P:(t + 1) * P], P)
                last.then_inc(avtr_ps, 1)
                pe.wait_ge(sw_ready, at(j, 1, 1))
                mm(wk[3][:, 0:SEQ], ones, sw[:, 0:SEQ], start=True, stop=False)
                mm(wk[3][:, P:SEQ], ones, sw[:, SEQ:384], start=False, stop=True).then_inc(den_ps, 1)
                for e in range(EC):
                    mm(wk[0][:, e * SEQ:(e + 1) * SEQ], mv_nat[:, 0, e * P:(e + 1) * P], sw[:, 0:SEQ], start=True, stop=False)
                    last = mm(wk[0][:, e * SEQ + P:(e + 1) * SEQ], mv_nat[:, 1, e * P:(e + 1) * P], sw[:, SEQ:384],
                              start=False, stop=True)
                last.then_inc(num_ps, 1)
                pe.wait_ge(qm_ready, at(j, 1, 1))
                pe.wait_ge(vnat_ready, at(j, 1, 1))
                query_states(range(CSLOTS))
                pe.wait_ge(mvlo_ready, at(j, 1, 1))
                value_rows(0, wk[1])
                chunk(11)
                pe.wait_ge(h_ready, at(j, 1, 1))
                value_rows(1, wk[3])
                pe.wait_ge(va_ready, at(j, 1, 1))
                for d in range(EC):
                    for t in range(2):
                        last = mm(wk[0][:, d * MHD:(d + 1) * MHD], mk_nat[:, t, d * P:(d + 1) * P], va[:, t, :],
                                  start=(t == 0), stop=(t == 1))
                last.then_inc(cn_ps, 1)
                chunk(12)
                pe.wait_ge(ctmp_ready, at(j, 8, 2))
                for t in range(2):
                    col = SEQ - 1 if t == 0 else 383
                    last = mm(wk[1][0:1, 0:MHD], wt[:, col:col + 1], mk_nat[:, t, :], start=(t == 0), stop=(t == 1))
                last.then_inc(cn_ps, 1)
                pe.wait_ge(ctmp_ready, at(j, 8, 4))
                prob_sums(0, wk[3])
                pe.wait_ge(cn_ready, at(j, 2, 2))
                prompt_scores(0)
                pe.wait_ge(g_read, at(j, 2, 1))
                cached_values(0, (0, 1))
                pe.wait_ge(l_read, at(j, 2, 1))
                prompt_scores(1)
                chunk(13)
                cached_values(0, (2, 3))
                for i in range(2):
                    bank = wk[1 + 2 * i]
                    pe.wait_ge(p_ready, at(j, 2, i + 1))
                    tr(bank[:, 0:P], att[:, i, 0:P], P)
                    tr(bank[:, P:SEQ], att[:, i, P:SEQ], P)
                    tr(bank[:, SEQ:384], att[:, i, SEQ:384], P).then_inc(ptr_ps, 1)
                block_sums(1, wk[0])
                cached_values(0, (4, 5))
                pe.wait_ge(g_read, at(j, 2, 2))
                value_rows(2, wk[0])
                for i in range(2):
                    bank = wk[1 + 2 * i]
                    pe.wait_ge(pT_ready, at(j, 2, i + 1))
                    mm(bank[:, 0:SEQ], v_nat[:, 0, i * P:(i + 1) * P], pT[:, i, 0:SEQ], start=True, stop=False)
                    mm(bank[:, P:SEQ], v_nat[:, 1, i * P:(i + 1) * P], pT[:, i, SEQ:384], start=False, stop=True)\
                        .then_inc(pvh_ps, 1)
                cached_values(0, (6, 7))
                query_states(range(CSLOTS, NB))
                for g in range(2):
                    for d in range(EC):
                        last = mm(wk[2][0:NB, MHD + g:MHD + g + 1], qprod[:, g, d, :], ones[:, 0:1],
                                  start=False, stop=(d == EC - 1), skip_group_check=True)
                last.then_inc(qc_ps, 1)
                chunk(14)
                pe.wait_ge(ctmp_ready, at(j, 8, 6))
                pe.wait_ge(hs_ready, at(j, 1, 1))
                for e in range(EC):
                    last = columns_of(wk[0][:, e * NB:(e + 1) * NB], hs[:, e * P:(e + 1) * P], ident[0:NB, 0:NB])
                last.then_inc(hst_ps, 1)
                cached_values(1, (0, 1))
                pe.wait_ge(qc_read, at(j, 1, 1))
                value_rows(3, wk[2])
                pe.wait_ge(attg_ready, at(j, 2, 2))
                prob_sums(1, wk[1])
                cached_values(1, (2, 3))
                pe.wait_ge(sqh_ready, at(j, 1, 1))
                for e in range(EC):
                    last = mm(wk[3][:, 0:T], ones, sq[:, e, :], start=(e == 0), stop=(e == 1))
                last.then_inc(mln_ps, 1)
                sample_columns(wk[0])
                chunk(15)
                cached_values(1, range(4, PAGES))

            banks = pj + pa
            pe.wait_ge(evac, at(JOBS, CHUNKS, 0, HEADS))

            def sample_tokens():
                pe.wait_ge(accr_ready, 2 * JOBS + 1)
                sample_columns(wk[2])
                pe.wait_ge(ep_dve, 1)
                mm(wk[0][:, 0:64], ones, epi[:, 0, :], start=True, stop=True)
                tr(wk[1][0:64, 0:P], kTs[:, :, :].rearrange("p h b -> p (h b)"), P)
                tr(wk[1][0:64, P:2 * P], vTs[:, :, :].rearrange("p h b -> p (h b)"), P).then_inc(ep_ps, 1)

            def y_rows(c):
                pe.wait_ge(yT_ready, c + 1)
                if c >= 4:
                    pe.wait_ge(ep_y, c - 3)
                for t in range(2):
                    tr(wk[c % 4][:, t * P:(t + 1) * P], yT[:, c % 2, t * P:(t + 1) * P], P)
                tr(wk[c % 4][0:NB, 2 * P:3 * P], yT[:, c % 2, SEQ:T], P).then_inc(y_ps, 1)

            for i in range(5 * KC):
                m, c = i // KC, i % KC
                if i == 2:
                    sample_tokens()
                if i >= 4:
                    b = i - 4
                    pe.wait_ge(*((sg_ready, b + 1) if b < 2 * KC else (ywk, b - 2 * KC + 1) if b < 4 * KC else (yT_ready, b - 4 * KC + 1)))
                if c == 0 and m in (2, 3):
                    pe.wait_ge(a2_lo, m - 1)
                if i == 4 * KC:
                    pe.wait_ge(ep_dve, 3)
                    pe.wait_ge(ep_act, 2)
                project(banks[i % 4], i % WSPLIT, (xn2, xn2, att2, mlg2, mrg2)[m], at(JOBS, CHUNKS, i + 1, HEADS),
                        parts=mrg_lo if i == 4 * KC else None)
                if i > 4 * KC:
                    y_rows(i - 4 * KC - 1)
            y_rows(KC - 1)

        @block.scalar
        def _(act):
            A = nc.scalar.activation
            ch = Chain(act, act_step)
            act.sem_inc(mrs_ready, 1)
            for s in cstore:
                act.sem_inc(s, 16)
            for s in (st_k, st_v, st_c, st_n, st_ns):
                act.sem_inc(s, 16)
            nc.scalar.preload_act_table_set("natural_log_exp_and_others")

            act.wait_ge(boot_x, 48)
            act.wait_ge(boot, 96)
            for t in range(3):
                R = P if t < 2 else NB
                ch.link(A(yout[0:R, t, :], xin[0:R, t, :], ACT.Square, accum_out=ssx[0:R, t, 0:1]))
                ch.link(A(ssx[0:R, t, 1:2], ssx[0:R, t, 0:1], ACT.Ln, scale=1.0 / D, bias=epsc[0:R, :]))
                A(ssx[0:R, t, 2:3], ssx[0:R, t, 1:2], ACT.Exp, scale=-0.5).then_inc(xss, 1)

            def split_hi(j, c):
                pair = c // 2
                act.wait_ge(wload[pair % WRAW], at(j, 64, 16 * (pair // WRAW + 3)))
                act.wait_ge(proj, at(j, CHUNKS, c + 1 - WSPLIT, HEADS))
                A(w2[:, c % WSPLIT, 0], wraw[:, pair % WRAW, :, (c % 2) * P:(c % 2 + 1) * P], ACT.Copy).then_inc(whi_ready, 1)

            def first_hi(h):
                act.wait_ge(wload[(h // 2) % WRAW], 16 * (h // 2 // WRAW + 1))
                if h >= WSPLIT:
                    act.wait_ge(proj, h + 1 - WSPLIT)
                A(w2[:, h % WSPLIT, 0], wraw[:, (h // 2) % WRAW, :, (h % 2) * P:(h % 2 + 1) * P], ACT.Copy).then_inc(whi_ready, 1)

            for k in range(KC):
                if k % 2 == 0:
                    act.wait_ge(xt_ps, k + 1)
                    A(xnT[:, k, :], wk[k % 4][:, 0:T], ACT.Copy, scale=normw[:, k:k + 1]).then_inc(xt_even, 1)
                    act.wait_ge(xt_even, k // 2 + 1)
                else:
                    act.wait_ge(xt_odd, k // 2 + 1)
                A(xn2[:, 0, k, :], xnT[:, k, :], ACT.Copy).then_inc(xhi_ready, 1)
                if k == 3:
                    first_hi(0)
            first_hi(1)
            first_hi(2)
            for g in range(2):
                act.wait_ge(gate_ps, g + 1)
                A(gr[:, g, :], wk[g][0:MH, 0:T], ACT.Identity, bias=bg[:, g:g + 1]).then_inc(gate_raw, 1)

            def head_copy(c, dst, w, i):
                act.wait_ge(proj, c)
                A(dst, pj[i][:, 0:T], ACT.Copy, scale=w)
                A(sq[:, i, :], pj[i][:, 0:T], ACT.Square).then_inc(evac, 1)

            def inv_rms(ss, dst, width, chain):
                chain.link(A(dst, ss, ACT.Ln, scale=1.0 / width, bias=epsc))
                return A(dst, dst, ACT.Exp, scale=-0.5)

            for h in range(HEADS + 1):
                if h < HEADS:
                    if h + AHEAD < HEADS:
                        first_hi(h + AHEAD)
                    else:
                        split_hi(0, h + AHEAD - HEADS)
                    if h >= 2:
                        act.wait_ge(norm_ps, h - 1)
                    head_copy(h + 1, qT[:, h, :], qkw[:, 0:1], h % 2)
                if h == 1:
                    act.wait_ge(gate_e, 1)
                    ch.link(A(gr[:, 3, :], gr[:, 3, :], ACT.Exp))
                    A(gr[:, 3, :], gr[:, 3, :], ACT.Ln, bias=1.0).then_inc(gate_ln, 1)
                if h == 6:
                    act.wait_ge(wN_in, 1)
                    A(wN[:, :, :], gN[:, 3:6, :], ACT.Exp).then_inc(wN_ready, 1)
                if h >= 1:
                    g = h - 1
                    act.wait_ge(norm_ps, g + 1)
                    if g >= 2:
                        act.wait_ge(q_ready, g - 1)
                    inv_rms(wk[2 * (g % 2)][:, 0:T], rs[:, g % 2, :], HD, ch).then_inc(rs_ready, 1)
            act.dma_start(o["m_p"], gr[:, 4, SEQ - 1:SEQ]).then_inc(st_misc, 16)
            act.dma_start(o["m_s"][0], msnew[:, :]).then_inc(st_misc, 16)
            act.wait_ge(boot_done, 1)
            act.wait_ge(st_misc, 32)
            pro = ch.n

            with act.Fori(0, JOBS) as j:
                ch.base, ch.n = at(j, ACT_STEPS, pro), 0

                def copy_chunk(c, dst, scale=1.0):
                    split_hi(j, c + AHEAD)
                    act.wait_ge(proj, at(j, CHUNKS, c + 1, HEADS))
                    A(dst, pj[c % 2][:, 0:T], ACT.Copy, scale=scale).then_inc(evac, 1)

                def outer_rows(b, bank):
                    if b >= 2:
                        act.wait_ge(c_ready, at(j, NB, b - 1))
                    for d in range(EC):
                        last = A(ctmp[:, b % 2, d, :], bank[:, (b % 2) * MHD:(b % 2 + 1) * MHD], ACT.Copy, scale=kc[:, d, b:b + 1])
                    last.then_inc(ctmp_ready, 1)

                def cache_probs(odd):
                    act.wait_ge(pm_ready, at(j, 2, odd + 1))
                    A(prob[:, odd], prob[:, odd], ACT.Exp, scale=SCALE).then_inc(prob_ready, 1)

                def load_state(b):
                    act.wait_ge(cstore[b % CSLOTS], at(j, 32, 16 * (b // CSLOTS + 1)))
                    act.dma_start(cslot[:, b % CSLOTS], a["state_mlstm_C"][0, b, ds(j, 1), :, :].rearrange(
                        "o (c p) e -> p (o c) e", p=P)).then_inc(cload[b % CSLOTS], 16)

                def store_state(b):
                    act.wait_ge(c_ready, at(j, NB, b + 1))
                    act.dma_start(o["C_s"][0, b, ds(j, 1), :, :].rearrange("o (c p) e -> p (o c) e", p=P),
                                  cslot[:, b % CSLOTS]).then_inc(cstore[b % CSLOTS], 16)

                split_hi(j, AHEAD)
                head_copy(at(j, CHUNKS, 1, HEADS), kT[:, 0, :], qkw[:, 1:2], 0)
                act.wait_ge(accr_ready, at(j, 2, 1))
                for i in range(4):
                    act.wait_ge(qbc_ps, at(j, 4, i + 1))
                    A(qbc[:, i // 2, (i % 2) * 512:(i % 2 + 1) * 512], wk[i][:, :], ACT.Copy).then_inc(qbc_ready, 1)
                split_hi(j, 1 + AHEAD)
                head_copy(at(j, CHUNKS, 2, HEADS), kT[:, 1, :], qkw[:, 1:2], 1)
                copy_chunk(2, mqT[:, 0, :])
                act.wait_ge(mlg_ready, at(j, 1, 1))
                for i in range(2):
                    act.wait_ge(norm_ps, at(j, 2, i + 1, HEADS))
                    inv_rms(wk[2 * i][:, 0:T], rs[:, i, :], HD, ch).then_inc(rs_ready, 1)
                copy_chunk(3, mqT[:, 1, :])
                for b in range(CSLOTS):
                    load_state(b)
                copy_chunk(4, mkT[:, 0, :], MHD ** -0.5)
                copy_chunk(5, mkT[:, 1, :], MHD ** -0.5)
                act.wait_ge(ktr_ps, at(j, 1, 1))
                act.wait_ge(st_k, at(j, 16, 16))
                A(k_nat[:, :, :].rearrange("p t c -> p (t c)"), wk[0][:, :], ACT.Copy).then_inc(knat_ready, 1)
                copy_chunk(6, rawT[:, 0, :])
                act.wait_ge(mktr_ps, at(j, 2, 1))
                A(mk_nat[:, :, :].rearrange("p t c -> p (t c)"), wk[1][:, :], ACT.Copy).then_inc(mk_ready, 1)
                act.wait_ge(mktr_ps, at(j, 2, 2))
                A(mks[:, :], wk[2][0:NB, 0:MHD], ACT.Copy).then_inc(mk_ready, 1)
                copy_chunk(7, rawT[:, 1, :])
                act.wait_ge(st_ns, at(j, 16, 16))
                copy_chunk(8, vT[:, 0, :])
                act.wait_ge(mvtr_ps, at(j, 2, 1))
                A(mv_nat[:, :, :].rearrange("p t c -> p (t c)"), wk[1][:, :], ACT.Copy).then_inc(mv_ready, 1)
                act.wait_ge(mvtr_ps, at(j, 2, 2))
                A(mvs[:, :], wk[2][0:NB, 0:MHD], ACT.Copy)
                A(mvs2[0:NB, :], wk[2][0:NB, 0:MHD], ACT.Copy).then_inc(mv_ready, 1)
                act.wait_ge(bc_ps, at(j, 1, 1))
                act.wait_ge(wl_ready, at(j, 1, 1))
                u = [uT[:, t, ds(j, 1)] for t in range(2)]
                A(wt[:, P:SEQ], wk[0][:, P:SEQ], ACT.Exp, bias=u[0])
                A(emt[:, :], wk[0][:, SEQ:2 * SEQ], ACT.Exp)
                A(wt[:, 0:P], wt[:, 0:P], ACT.Exp, bias=u[0])
                A(wt[:, SEQ:384], wt[:, SEQ:384], ACT.Exp, bias=u[1]).then_inc(w_ready, 1)
                copy_chunk(9, vT[:, 1, :])
                act.wait_ge(knat_ready, at(j, 1, 1))
                act.dma_start(o["k_p"][:, ds(j * 256, 256)].rearrange("(t p) c -> p t c", p=P), k_nat[:, :, :]).then_inc(st_k, 16)
                copy_chunk(10, zraw[:, 0, 0, :])
                act.wait_ge(avtr_ps, at(j, 1, 1))
                act.wait_ge(st_v, at(j, 16, 16))
                A(v_nat[:, :, :].rearrange("p t c -> p (t c)"), wk[2][:, :], ACT.Copy).then_inc(vnat_ready, 1)
                act.wait_ge(vbc_ps, at(j, 4, 1))
                outer_rows(0, wk[1])
                outer_rows(1, wk[1])
                cache_probs(0)
                copy_chunk(11, zraw[:, 0, 1, :])
                act.wait_ge(vbc_ps, at(j, 4, 2))
                outer_rows(2, wk[3])
                outer_rows(3, wk[3])
                act.wait_ge(cn_ps, at(j, 2, 1))
                A(cnew[:, :, :].rearrange("p c e -> p (c e)"), wk[0][:, :], ACT.Copy).then_inc(cn_ready, 1)
                copy_chunk(12, zraw[:, 2, 0, :])
                act.wait_ge(cn_ps, at(j, 2, 2))
                act.wait_ge(st_n, at(j, 16, 16))
                A(nnew[:, :], wk[1][0:1, 0:MHD], ACT.Copy).then_inc(cn_ready, 1)
                for b in range(CSLOTS):
                    store_state(b)
                act.wait_ge(cn_ready, at(j, 2, 2))
                act.dma_start(o["C_p"][0, 0, ds(j, 1), :, :].rearrange("o (c p) e -> p (o c) e", p=P),
                              cnew[:, :, :]).then_inc(st_c, 16)
                act.dma_start(o["n_p"][0, 0, ds(j, 1), :], nnew[:, :]).then_inc(st_n, 16)
                for i in range(2):
                    act.wait_ge(smax_ready, at(j, 2, i + 1))
                    A(att[:, i, 0:P], att[:, i, 0:P], ACT.Exp, scale=SCALE, bias=nm[:, i, 0:1], accum_out=rsum[:, i, 0:1])
                    A(att[:, i, P:384], att[:, i, P:384], ACT.Exp, scale=SCALE, bias=nm[:, i, 1:2],
                      accum_out=rsum[:, i, 1:2]).then_inc(att_exp, 1)
                copy_chunk(13, zraw[:, 2, 1, :])
                for i in range(2):
                    act.wait_ge(ptr_ps, at(j, 2, i + 1))
                    A(pT[:, i, :], wk[1 + 2 * i][:, 0:384], ACT.Copy).then_inc(pT_ready, 1)
                for b in range(CSLOTS, NB):
                    load_state(b)
                cache_probs(1)
                act.wait_ge(evac, at(j, CHUNKS, 14, HEADS))
                act.wait_ge(c_ready, at(j, NB, CSLOTS))
                A(zsig[:, 0], zraw[:, 0], ACT.Sigmoid).then_inc(sig_ready, 1)
                A(zraw[:, 2], zraw[:, 2], ACT.Sigmoid).then_inc(sig_ready, 1)
                act.wait_ge(silu_ready, at(j, 1, 1))
                act.wait_ge(vbc_ps, at(j, 4, 3))
                outer_rows(4, wk[0])
                outer_rows(5, wk[0])
                copy_chunk(14, zraw[:, 1, 0, :])
                act.wait_ge(vbc_ps, at(j, 4, 4))
                outer_rows(6, wk[2])
                outer_rows(7, wk[2])
                act.wait_ge(hmo_ready, at(j, 1, 1))
                A(sq[:, :, :], hT[:, :, :], ACT.Square).then_inc(sqh_ready, 1)
                copy_chunk(15, zraw[:, 1, 1, :])
                act.wait_ge(vnat_ready, at(j, 1, 1))
                act.dma_start(o["v_p"][:, ds(j * 256, 256)].rearrange("(t p) c -> p t c", p=P), v_nat[:, :, :]).then_inc(st_v, 16)
                for b in range(CSLOTS, NB):
                    store_state(b)
                act.wait_ge(nso_ready, at(j, 1, 1))
                act.dma_start(o["n_s"][0, :, ds(j, 1), :].rearrange("b o d -> b (o d)"), nso).then_inc(st_ns, 16)
                act.wait_ge(evac, at(j, CHUNKS, 16, HEADS))
                act.wait_ge(c_ready, at(j, NB, NB))
                A(zsig[:, 1], zraw[:, 1], ACT.Sigmoid).then_inc(sig_ready, 1)
                act.wait_ge(mln_ps, at(j, 1, 1))
                inv_rms(wk[3][:, 0:T], rs[:, 0, :], MHD, ch).then_inc(mrs_ready, 1)
                assert ch.n == ACT_STEPS, ("ACT_STEPS", ch.n)

            banks = pj + pa
            act.wait_ge(k_used, at(JOBS, 16, KSLOTS))
            act.wait_ge(v_used, at(JOBS, 16, VSLOTS))

            def rows_of_samples():
                act.wait_ge(ep_ps, 1)
                A(k_nat[0:64, 0, :], wk[1][0:64, 0:2 * P], ACT.Copy).then_inc(ep_act, 1)
                act.wait_ge(ep_act, 2)
                act.dma_start(o["k_s"], k_nat[0:64, 0, 0:P]).then_inc(st_misc, 16)
                act.dma_start(o["v_s"], k_nat[0:64, 0, P:2 * P]).then_inc(st_misc, 16)

            for i in range(5 * KC):
                m, c = i // KC, i % KC
                if i + AHEAD < 5 * KC:
                    split_hi(JOBS, i + AHEAD)
                if i == 1:
                    act.wait_ge(ep_dve, 3)
                    A(epi[:, 4:6, :], epi[:, 4:6, :], ACT.Exp, scale=SCALE).then_inc(ep_act, 1)
                    rows_of_samples()
                if i == KC:
                    act.wait_ge(ep_dve, 4)
                    A(att2[:, 0], qT[:, :, :], ACT.Copy).then_inc(a2_hi, 1)
                if i == 2 * KC:
                    act.wait_ge(proj, at(JOBS, CHUNKS, 2 * KC, HEADS))
                    A(mlg2[:, 0], mlg[:, :, :], ACT.Copy).then_inc(a2_hi, 1)
                if m < 2:
                    act.wait_ge(proj, at(JOBS, CHUNKS, i + 1, HEADS))
                    A((sga, sgm)[m][:, c, :], banks[i % 4][:, 0:T], ACT.Sigmoid).then_inc(sg_ready, 1)
                elif m == 3:
                    act.wait_ge(ywk, KC + c + 1)
                    A(mrg2[:, 0, c, :], sgm[:, c, :], ACT.Copy).then_inc(mrg_hi, 1)
                elif m == 4:
                    act.wait_ge(proj, at(JOBS, CHUNKS, i + 1, HEADS))
                    if c >= 2:
                        act.wait_ge(y_ps, c - 1)
                    A(yT[:, c % 2, :], banks[i % 4][:, 0:T], ACT.Copy).then_inc(yT_ready, 1)

        @block.vector
        def _(dve):
            V = nc.vector
            ch = Chain(dve, dve_step)
            dve.wait_ge(boot_x, 48)
            for t in range(3):
                R = P if t < 2 else NB
                dve.wait_ge(xss, t + 1)
                V.tensor_scalar(xin[0:R, t, :], xin[0:R, t, :], ssx[0:R, t, 2:3], None, ALU.mult).then_inc(x_scaled, 1)

            def lo(q, slot, half):
                V.tensor_tensor(w2[:, q, 1], wraw[:, slot, :, half * P:(half + 1) * P], w2[:, q, 0], ALU.subtract).then_inc(wlo_ready, 1)

            def split_lo(j, c):
                dve.wait_ge(whi_ready, at(j, CHUNKS, c + 1, HEADS))
                lo(c % WSPLIT, (c // 2) % WRAW, c % 2)

            def first_lo(h):
                dve.wait_ge(whi_ready, h + 1)
                lo(h % WSPLIT, (h // 2) % WRAW, h % 2)

            for k in range(1, KC, 2):
                dve.wait_ge(xt_ps, k + 1)
                V.tensor_scalar(xnT[:, k, :], wk[k % 4][:, 0:T], normw[:, k:k + 1], None, ALU.mult).then_inc(xt_odd, 1)
                for i in (k - 1, k):
                    dve.wait_ge(xhi_ready, i + 1)
                    if i == k:
                        dve.wait_ge(xt_odd, k // 2 + 1)
                    V.tensor_tensor(xn2[:, 1, i, :], xnT[:, i, :], xn2[:, 0, i, :], ALU.subtract).then_inc(xlo_ready, 1)
                if k == 5:
                    first_lo(0)
            first_lo(1)
            first_lo(2)
            dve.sem_inc(v_used, VSLOTS)
            dve.wait_ge(gate_raw, 2)
            dve.sem_inc(k_used, KSLOTS)
            V.scalar_tensor_tensor(out=gr[:, 3, :], in0=gr[:, 1, :], scalar=-1.0, in1=gr[:, 1, :], op0=ALU.mult, op1=ALU.min).then_inc(gate_e, 1)
            dve.wait_ge(nt_ps, 1)
            V.tensor_copy(nT[:, :, :, :], wk[2][:, 0:64]).then_inc(bcg_ps, 1)

            ch.link(V.tensor_scalar(accr[:, :], cst[0:HEADS, 0:HD], 0.0, None, ALU.mult))
            dve.sem_inc(accr_ready, 1)
            for t, n in ((qs2, D), (rows2, 2 * SEQ), (mvs2, MHD), (eye2, NB), (selc, 3)):
                ch.link(V.tensor_scalar(t[:, :], cst[0:LO + NB, 0:n], 0.0, None, ALU.mult))
            for row in (0, LO):
                ch.step(V.tensor_copy(eye2[row:row + NB, :], ident[row:row + NB, row:row + NB]))

            def rope_norm(x, r, ro, done):
                ch.step(V.tensor_tensor(hT[:, 0, :], ro[:, 0:T], sin, ALU.mult))
                ch.link(V.tensor_tensor(x, x, cos, ALU.mult))
                ch.link(V.tensor_tensor(x, x, hT[:, 0, :], ALU.add))
                V.tensor_tensor(x, x, r, ALU.mult).then_inc(done, 1)

            for h in range(HEADS):
                if h + AHEAD < HEADS:
                    first_lo(h + AHEAD)
                else:
                    split_lo(0, h + AHEAD - HEADS)
                dve.wait_ge(norm_ps, h + 1)
                dve.wait_ge(rs_ready, h + 1)
                rope_norm(qT[:, h, :], rs[:, h % 2, :], wk[2 * (h % 2) + 1], q_ready)
                dve.wait_ge(q_ready, h + 1)
                if h == 1:
                    dve.wait_ge(gate_ln, 1)
                    ch.link(V.tensor_scalar(gr[:, 1, :], gr[:, 1, :], 0.0, None, ALU.min))
                    ch.link(V.tensor_tensor(gr[:, 1, :], gr[:, 1, :], gr[:, 3, :], ALU.subtract))
                    ch.link(V.tensor_tensor_scan(gr[:, 3, 0:SEQ], ones[0:MH, 0:1].broadcast_to([MH, SEQ]), gr[:, 1, 0:SEQ], 0.0, ALU.mult, ALU.add))
                    ch.link(V.tensor_tensor(gr[:, 2, 0:SEQ], gr[:, 0, 0:SEQ], gr[:, 3, 0:SEQ], ALU.subtract))
                    ch.link(V.tensor_tensor_scan(gr[:, 5, 0:SEQ], ones[0:MH, 0:1].broadcast_to([MH, SEQ]), gr[:, 2, 0:SEQ], 0.0, ALU.mult, ALU.max))
                    ch.link(V.tensor_tensor(gr[:, 4, 0:SEQ], gr[:, 3, 0:SEQ], gr[:, 5, 0:SEQ], ALU.add))
                    ch.step(V.tensor_scalar(rows[:, 0, :], gr[:, 5, 0:SEQ], -1.0, None, ALU.mult))
                    ch.link(V.tensor_scalar(rows[:, 1, :], gr[:, 4, 0:SEQ], -1.0, None, ALU.mult))
                    dve.sem_inc(rows_ready, 1)
                    flat = rows[:, :, :].rearrange("p a t -> p (a t)")
                    ch.link(V.tensor_copy(rows2[0:MH, :], flat))
                    ch.link(V.tensor_tensor(rows2[LO:LO + MH, :], flat, rows2[0:MH, :], ALU.subtract))
                if h == 4:
                    dve.wait_ge(gtr_ps, 1)
                    ch.step(V.tensor_copy(uT[:, :, :], pa[0][:, 0:2 * MH]))
                    ch.link(V.tensor_copy(gN[:, 0:2, :], pa[1][0:NB, 0:2 * MH]))
                    ch.link(V.tensor_tensor(gN[:, 2, :], gN[:, 1, :], mstate[:, :], ALU.add))
                    ch.link(V.tensor_tensor(msnew[:, :], gN[:, 2, :], gN[:, 0, :], ALU.max))
                    ch.step(V.tensor_tensor(gN[:, 3, :], gN[:, 2, :], msnew[:, :], ALU.subtract))
                    ch.step(V.tensor_tensor(gN[:, 4, :], gN[:, 0, :], msnew[:, :], ALU.subtract))
                    V.tensor_scalar(gN[:, 5, :], msnew[:, :], -1.0, None, ALU.mult).then_inc(wN_in, 1)
                if h == 6:
                    dve.wait_ge(wN_ready, 1)
                    V.tensor_tensor(gexp[:, :, :], wN[:, :, :].rearrange("p g h -> p (g h)").unsqueeze(2).broadcast_to([NB, 12, NB]),
                                    ident[0:NB, 0:NB].unsqueeze(1).broadcast_to([NB, 12, NB]), ALU.mult).then_inc(gexp_ready, 1)
            ch.step(V.tensor_copy(qTs[:, :, :], qT[:, :, SEQ:T]))
            dve.wait_ge(qs_ps, 1)
            for half in range(2):
                cut = slice(half * 512, (half + 1) * 512)
                ch.link(V.tensor_copy(qs2[0:NB, cut], wk[2 + half][0:NB, :]))
                ch.link(V.tensor_tensor(qs2[LO:LO + NB, cut], wk[2 + half][0:NB, :], qs2[0:NB, cut], ALU.subtract))
            dve.wait_ge(bcg_ps, 2)
            ch.link(V.tensor_copy(bcg[:, :, :, :], pa[0][:, 64:160]))
            dve.sem_inc(boot_done, 1)
            dve.sem_inc(mlg_ready, 1)
            pro = ch.n

            def sample_out(n, slot, bank):
                dve.wait_ge(acct_ps, n)
                V.tensor_copy(accS[:, ds(slot, 1), :].rearrange("p o h -> p (o h)"), bank[:, 0:HEADS]).then_inc(acc_ready, 1)

            def select_rows(j):
                for row in (0, LO):
                    ch.step(V.tensor_copy(selc[row:row + NB, 2:3], ident[row:row + NB, ds(j + row, 1)]))
                    ch.step(V.tensor_copy(selc[row:row + NB, 0:2], ident[row:row + NB, ds(j * 2 + row, 2)]))
                dve.wait_ge(dve_step, ch.base + ch.n)
                dve.sem_inc(selc_ready, 1)

            select_rows(0)
            pro = ch.n

            with dve.Fori(0, JOBS) as j:
                ch.base, ch.n = at(j, DVE_STEPS, pro), 0

                def page(s):
                    odd, pg = s // PAGES, s % PAGES
                    if pg == 0:
                        dve.wait_ge(qbc_ready, at(j, 4, 2 * odd + 2))
                    dve.wait_ge(kload[pg % KSLOTS], at(j, 64, 16 * (2 * odd + pg // KSLOTS + 1)))
                    for h in range(HEADS):
                        k = kpages[:, pg % KSLOTS, h * HD:(h + 1) * HD]
                        last = V.tensor_tensor_reduce(k, k, qbc[:, odd, h * HD:(h + 1) * HD], 1.0, 0.0, ALU.mult, ALU.add,
                                                      sco[:, odd, pg, h:h + 1])
                    last.then_inc(k_used, 1)

                def select(odd, bank):
                    g4, rk, cmp, cap = (gsm[:, odd, i, :].rearrange("p (n h) -> p n h", n=NBLK) for i in range(4))
                    dve.wait_ge(g_ps, at(j, 2, odd + 1))
                    V.tensor_reduce(g4, bank[:, 0:64].rearrange("p (n q h) -> p n h q", n=NBLK, q=PPB), AX.X, ALU.add).then_inc(g_read, 1)
                    dve.wait_ge(g_read, at(j, 2, odd + 1))
                    prev = rank0
                    for k in range(1, NBLK):
                        n = NBLK - k
                        ch.link(V.tensor_tensor(cmp[:, 0:n], g4[:, 0:n], g4[:, k:NBLK], ALU.is_ge))
                        if k == 1:
                            ch.step(V.tensor_copy(rk[:, 0:1], prev[:, 0:1]))
                            ch.link(V.tensor_tensor(rk[:, k:NBLK], prev[:, k:NBLK], cmp[:, 0:n], ALU.add))
                        else:
                            ch.link(V.tensor_tensor(rk[:, k:NBLK], rk[:, k:NBLK], cmp[:, 0:n], ALU.add))
                        ch.link(V.tensor_tensor(rk[:, 0:n], rk[:, 0:n], cmp[:, 0:n], ALU.subtract))
                    ch.link(V.tensor_scalar(cmp, rk, float(TOPK), 2 * BIG, ALU.is_lt, ALU.mult))
                    ch.link(V.tensor_scalar(cap, cmp, -BIG, None, ALU.add))
                    s4 = sco[:, odd].rearrange("p (n q) h -> p n q h", q=PPB)
                    ch.link(V.tensor_tensor(s4, s4, cap.unsqueeze(2).broadcast_to([P, NBLK, PPB, HEADS]), ALU.min))
                    V.tensor_reduce(mx[:, odd, :], sco[:, odd].rearrange("p a h -> p h a"), AX.X, ALU.max).then_inc(mx_ready, 1)

                def shifted(odd):
                    dve.wait_ge(gmax_ready, at(j, 2, odd + 1))
                    ch.step(V.tensor_copy(gmax[:, ds(j * 2 + odd, 1), :].rearrange("p o h -> p (o h)"), gm[:, odd, :]))
                    V.tensor_tensor(prob[:, odd], sco[:, odd],
                                    gm[:, odd, :].unsqueeze(1).broadcast_to([P, PAGES, HEADS]), ALU.subtract).then_inc(pm_ready, 1)

                def prob_sums(odd, bank):
                    dve.wait_ge(l_ps, at(j, 2, odd + 1))
                    V.tensor_reduce(lsum[:, ds(j * 2 + odd, 1), :].rearrange("p o h -> p (o h)"),
                                    bank[:, 0:64].rearrange("p (a h) -> p h a", a=PAGES), AX.X, ALU.add).then_inc(l_read, 1)

                def diagonal(odd):
                    dve.wait_ge(v_used, at(j, 16, 8 * odd + 8, VSLOTS))
                    for half in range(2):
                        n = HEADS // 2
                        ch.step(V.tensor_tensor(accd[:, half * n:(half + 1) * n, :],
                                                pa[half][0:HEADS, :].rearrange("p (h d) -> p h d", h=n),
                                                ident[0:HEADS, half * n:(half + 1) * n].unsqueeze(2).broadcast_to([HEADS, n, HD]),
                                                ALU.mult))
                    dve.wait_ge(dve_step, ch.base + ch.n)
                    V.tensor_reduce(accr[:, :], accd[:, :, :].rearrange("p h d -> p d h"), AX.X, ALU.add).then_inc(accr_ready, 1)

                def new_state(b):
                    dve.wait_ge(ctmp_ready, at(j, 8, b + 1))
                    dve.wait_ge(qc_ps, at(j, 3, b // CSLOTS + 1))
                    V.scalar_tensor_tensor(out=cslot[:, b % CSLOTS], in0=cslot[:, b % CSLOTS],
                                           scalar=bcg[:, 0, ds(j, 1), b:b + 1].rearrange("p o c -> p (o c)"),
                                           in1=ctmp[:, b % 2], op0=ALU.mult, op1=ALU.add).then_inc(c_ready, 1)

                dve.wait_ge(mrs_ready, at(j, 1, 1))
                ch.step(V.tensor_copy(qTc[:, :, :], qT[:, ds(j * 2, 2), :]))
                ch.step(V.tensor_copy(w3[:, :], wN[:, :, ds(j, 1)].rearrange("p g o -> p (g o)")))
                split_lo(j, 0 + AHEAD)
                page(0)
                page(1)
                page(2)
                split_lo(j, 1 + AHEAD)
                page(3)
                split_lo(j, 2 + AHEAD)
                page(4)
                page(5)
                sample_out(at(j, 2, 1), j * 2, pa[0])
                for i in range(2):
                    dve.wait_ge(norm_ps, at(j, 2, i + 1, HEADS))
                    dve.wait_ge(rs_ready, at(j, 2, i + 1, HEADS))
                    rope_norm(kT[:, i, :], rs[:, i, :], wk[2 * i + 1], kT_ready)
                    dve.wait_ge(kT_ready, at(j, 2, i + 1))
                ch.step(V.tensor_copy(kTs[:, ds(j * 2, 2), :], kT[:, :, SEQ:T]))
                split_lo(j, 3 + AHEAD)
                page(6)
                split_lo(j, 4 + AHEAD)
                page(7)
                split_lo(j, 5 + AHEAD)
                page(8)
                dve.wait_ge(bc_ps, at(j, 1, 1))
                ch.step(V.tensor_tensor(wt[:, 0:P], wk[0][:, 0:P], triT, ALU.add))
                V.tensor_tensor(wt[:, SEQ:384], wk[0][:, P:SEQ], triT, ALU.add).then_inc(wl_ready, 1)
                page(9)
                select(0, pa[0])
                split_lo(j, 6 + AHEAD)
                page(10)
                split_lo(j, 7 + AHEAD)
                page(11)
                dve.wait_ge(st_ps, at(j, 1, 1))
                dve.wait_ge(w_ready, at(j, 1, 1))
                V.tensor_tensor(sw[:, :], wk[3][:, 0:384], wt[:, :], ALU.mult).then_inc(sw_ready, 1)
                for d in range(EC):
                    ch.step(V.tensor_tensor(qmask[:, d], mqT[:, d, SEQ:T].unsqueeze(1).broadcast_to([P, NB, NB]), delta, ALU.mult))
                ch.step(V.tensor_tensor(qprod[:, 0], nT[:, ds(j, 1), :, :].rearrange("p o c b -> p (o c) b"), mqT[:, :, SEQ:T], ALU.mult))
                ch.step(V.tensor_tensor(kc[:, :, :], mkT[:, :, SEQ:T], bcg[:, 1, ds(j, 1), :].broadcast_to([P, EC, NB]), ALU.mult))
                V.tensor_tensor(qprod[:, 1], mkT[:, :, SEQ:T], mqT[:, :, SEQ:T], ALU.mult).then_inc(qm_ready, 1)
                dve.wait_ge(mv_ready, at(j, 2, 2))
                V.tensor_tensor(mvs2[LO:LO + NB, :], mvs[:, :], mvs2[0:NB, :], ALU.subtract).then_inc(mvlo_ready, 1)
                split_lo(j, 8 + AHEAD)
                dve.wait_ge(evac, at(j, CHUNKS, 10, HEADS))
                ch.step(V.tensor_copy(vTs[:, ds(j * 2, 2), :], vT[:, :, SEQ:T]))
                dve.wait_ge(mv_ready, at(j, 2, 1))
                for t in range(2):
                    col = SEQ - 1 if t == 0 else 383
                    if t == 0:
                        dve.wait_ge(st_c, at(j, 16, 16))
                    last = V.tensor_scalar(va[:, t, :], mv_nat[:, t, :], wt[:, col:col + 1], None, ALU.mult)
                last.then_inc(va_ready, 1)
                page(12)
                shifted(0)
                split_lo(j, 9 + AHEAD)
                page(13)
                split_lo(j, 10 + AHEAD)
                dve.wait_ge(den_ps, at(j, 1, 1))
                ch.link(V.tensor_tensor(dn[:, :], wk[3][:, 0:SEQ], emt[:, :], ALU.max))
                ch.link(V.scalar_tensor_tensor(out=dn[:, :], in0=wk[3][:, 0:SEQ], scalar=-1.0, in1=dn[:, :],
                                               op0=ALU.mult, op1=ALU.max))
                ch.link(V.reciprocal(dn[:, :], dn[:, :]))
                dve.wait_ge(num_ps, at(j, 1, 1))
                V.tensor_tensor(hT[:, :, 0:SEQ], wk[0][:, :].rearrange("p (e t) -> p e t", e=EC),
                                dn[:, :].unsqueeze(1).broadcast_to([P, EC, SEQ]), ALU.mult).then_inc(h_ready, 1)
                new_state(0)
                new_state(1)
                page(14)
                new_state(2)
                new_state(3)
                prob_sums(0, wk[3])
                split_lo(j, 11 + AHEAD)
                for i in range(2):
                    dve.wait_ge(sc_ps, at(j, 2, i + 1))
                    ch.link(V.tensor_tensor(att[:, i, :], wk[1 + 2 * i][:, 0:384], mask3, ALU.add))
                    ch.step(V.tensor_reduce(nm[:, i, 0:1], att[:, i, 0:P], AX.X, ALU.max))
                    ch.link(V.tensor_reduce(nm[:, i, 1:2], att[:, i, P:384], AX.X, ALU.max))
                    V.tensor_scalar(nm[:, i, :], nm[:, i, :], -SCALE, None, ALU.mult).then_inc(smax_ready, 1)
                page(15)
                split_lo(j, 12 + AHEAD)
                for i in range(2):
                    dve.wait_ge(att_exp, at(j, 2, i + 1))
                    ch.link(V.reciprocal(rsum[:, i, :], rsum[:, i, :]))
                    ch.step(V.tensor_scalar(att[:, i, 0:P], att[:, i, 0:P], rsum[:, i, 0:1], None, ALU.mult))
                    V.tensor_scalar(att[:, i, P:384], att[:, i, P:384], rsum[:, i, 1:2], None, ALU.mult).then_inc(p_ready, 1)
                select(1, wk[0])
                split_lo(j, 13 + AHEAD)
                shifted(1)
                dve.wait_ge(sig_ready, at(j, 3, 1))
                V.tensor_tensor(zraw[:, 0], zraw[:, 0], zsig[:, 0], ALU.mult).then_inc(silu_ready, 1)
                dve.wait_ge(silu_ready, at(j, 1, 1))
                ch.step(V.tensor_copy(qT[:, ds(j * 2, 2), SEQ:T], zraw[:, 0, :, SEQ:T]))
                diagonal(0)
                dve.wait_ge(qc_ps, at(j, 3, 3))
                ch.link(V.tensor_scalar(sm1[:, 0:1], wk[2][0:NB, MHD + 1:MHD + 2], w3[:, 1:2], None, ALU.mult))
                ch.link(V.scalar_tensor_tensor(out=sm1[:, 1:2], in0=wk[2][0:NB, MHD:MHD + 1], scalar=w3[:, 0:1], in1=sm1[:, 0:1],
                                               op0=ALU.mult, op1=ALU.add))
                ch.link(V.tensor_tensor(sm1[:, 2:3], sm1[:, 1:2], w3[:, 2:3], ALU.max))
                ch.link(V.scalar_tensor_tensor(out=sm1[:, 2:3], in0=sm1[:, 1:2], scalar=-1.0, in1=sm1[:, 2:3],
                                               op0=ALU.mult, op1=ALU.max))
                ch.link(V.reciprocal(sm1[:, 3:4], sm1[:, 2:3]))
                V.tensor_scalar(hs[:, :], wk[2][0:NB, 0:MHD], w3[:, 0:1], None, ALU.mult).then_inc(qc_read, 1)
                dve.wait_ge(qc_read, at(j, 1, 1))
                dve.wait_ge(mv_ready, at(j, 2, 2))
                ch.link(V.scalar_tensor_tensor(out=hs[:, :], in0=mvs[:, :], scalar=sm1[:, 0:1], in1=hs[:, :], op0=ALU.mult, op1=ALU.add))
                V.tensor_scalar(hs[:, :], hs[:, :], sm1[:, 3:4], None, ALU.mult).then_inc(hs_ready, 1)
                dve.wait_ge(mk_ready, at(j, 2, 2))
                ch.link(V.tensor_scalar(nso, mks[:, :], w3[:, 1:2], None, ALU.mult))
                V.scalar_tensor_tensor(out=nso, in0=nnat[:, ds(j * MHD, MHD)], scalar=w3[:, 0:1], in1=nso,
                                       op0=ALU.mult, op1=ALU.add).then_inc(nso_ready, 1)
                for i in range(2):
                    dve.wait_ge(pvh_ps, at(j, 2, i + 1))
                    V.tensor_tensor(qT[:, ds(j * 2 + i, 1), 0:SEQ].rearrange("p o t -> p (o t)"), wk[1 + 2 * i][:, 0:SEQ],
                                    zraw[:, 0, i, 0:SEQ], ALU.mult).then_inc(attg_ready, 1)
                new_state(4)
                new_state(5)
                split_lo(j, 14 + AHEAD)
                dve.wait_ge(hst_ps, at(j, 1, 1))
                dve.wait_ge(sig_ready, at(j, 3, 2))
                ch.link(V.tensor_copy(hT[:, :, SEQ:T], wk[0][:, 0:EC * NB].rearrange("p (e b) -> p e b", e=EC)))
                V.tensor_tensor(hT[:, :, :], hT[:, :, :], zraw[:, 2], ALU.mult).then_inc(hmo_ready, 1)
                new_state(6)
                new_state(7)
                prob_sums(1, wk[1])
                split_lo(j, 15 + AHEAD)
                sample_out(at(j, 2, 2), j * 2 + 1, wk[0])
                select_rows(j + 1)
                dve.wait_ge(sig_ready, at(j, 3, 3))
                ch.step(V.tensor_tensor(zraw[:, 1], zraw[:, 1], zsig[:, 1], ALU.mult))
                dve.wait_ge(mrs_ready, at(j, 1, 2))
                for e in range(EC):
                    ch.step(V.scalar_tensor_tensor(out=hT[:, e, :], in0=hT[:, e, :], scalar=mhw[:, e:e + 1], in1=rs[:, 0, :],
                                                   op0=ALU.mult, op1=ALU.mult))
                dve.wait_ge(dve_step, ch.base + ch.n)
                V.tensor_tensor(mlg[:, ds(j * 2, 2), :], hT[:, :, :], zraw[:, 1], ALU.mult).then_inc(mlg_ready, 1)
                diagonal(1)
                assert ch.n == DVE_STEPS, ("DVE_STEPS", ch.n)

            ch.base, ch.n = JOBS * DVE_STEPS + pro, 0
            dve.wait_ge(dve_step, ch.base)
            E = [epi[:, i, :].rearrange("p (h b) -> p h b", h=HEADS) for i in range(8)]
            hb = "p b h -> p h b"

            def token_scores():
                V.tensor_tensor(E[0], qTs[:, :, :], kTs[:, :, :], ALU.mult).then_inc(ep_dve, 1)
                dve.wait_ge(ep_ps, 1)
                ch.link(V.tensor_copy(E[1], wk[0][:, 0:64].rearrange("p (h b) -> p h b", h=HEADS)))
                ch.link(V.tensor_tensor(E[2], E[1], gmax[:, :, :].rearrange(hb), ALU.max))
                ch.step(V.tensor_tensor(E[4], gmax[:, :, :].rearrange(hb), E[2], ALU.subtract))
                ch.link(V.tensor_tensor(E[5], E[1], E[2], ALU.subtract))
                dve.sem_inc(ep_dve, 2)

            def merged_samples():
                dve.wait_ge(ep_act, 1)
                ch.link(V.tensor_tensor(E[6], lsum[:, :, :].rearrange(hb), E[4], ALU.mult))
                ch.link(V.tensor_tensor(E[6], E[6], E[5], ALU.add))
                ch.link(V.reciprocal(E[6], E[6]))
                ch.step(V.tensor_tensor(E[7], accS[:, 1:NB + 1, :].rearrange(hb), E[4], ALU.mult))
                ch.link(V.tensor_tensor(E[3], vTs[:, :, :], E[5], ALU.mult))
                ch.link(V.tensor_tensor(E[7], E[7], E[3], ALU.add))
                ch.link(V.tensor_tensor(E[7], E[7], E[6], ALU.mult))
                ch.link(V.tensor_tensor(qT[:, :, SEQ:T], qT[:, :, SEQ:T], E[7], ALU.mult))
                dve.sem_inc(ep_dve, 1)

            banks = pj + pa
            sample_out(2 * JOBS + 1, NB, wk[2])
            token_scores()
            for i in range(5 * KC + 1):
                m, c = i // KC, i % KC
                if 3 * KC < i <= 4 * KC:
                    k = i - 3 * KC - 1
                    dve.wait_ge(mrg_hi, k + 1)
                    V.tensor_tensor(mrg2[:, 1, k, :], sgm[:, k, :], mrg2[:, 0, k, :], ALU.subtract).then_inc(mrg_lo, 1)
                ahead = AHEAD if i < 3 * KC else AHEAD - 1
                if i != 3 * KC and i + ahead < 5 * KC:
                    split_lo(JOBS, i + ahead)
                if i == 2:
                    merged_samples()
                if i == KC:
                    dve.wait_ge(a2_hi, 1)
                    V.tensor_tensor(att2[:, 1], qT[:, :, :], att2[:, 0], ALU.subtract).then_inc(a2_lo, 1)
                if i == 2 * KC:
                    dve.wait_ge(a2_hi, 2)
                    V.tensor_tensor(mlg2[:, 1], mlg[:, :, :], mlg2[:, 0], ALU.subtract).then_inc(a2_lo, 1)
                if m == 2:
                    dve.wait_ge(proj, at(JOBS, CHUNKS, i + 1, HEADS))
                    dve.wait_ge(sg_ready, c + 1)
                    V.tensor_tensor(sga[:, c, :], banks[i % 4][:, 0:T], sga[:, c, :], ALU.mult).then_inc(ywk, 1)
                elif m == 3:
                    dve.wait_ge(proj, at(JOBS, CHUNKS, i + 1, HEADS))
                    dve.wait_ge(sg_ready, KC + c + 1)
                    ch.link(V.tensor_tensor(sgm[:, c, :], banks[i % 4][:, 0:T], sgm[:, c, :], ALU.mult))
                    V.tensor_tensor(sgm[:, c, :], sga[:, c, :], sgm[:, c, :], ALU.add).then_inc(ywk, 1)
                if i > 4 * KC:
                    c = i - 4 * KC - 1
                    dve.wait_ge(y_ps, c + 1)
                    if c == 0:
                        dve.wait_ge(xres_load, 48)
                    for t in range(3):
                        M = P if t < 2 else NB
                        cut = slice(c * P, (c + 1) * P)
                        last = V.tensor_tensor(yout[0:M, t, cut], wk[c % 4][0:M, t * P:(t + 1) * P], xres[t][0:M, cut], ALU.add)
                    last.then_inc(ep_y, 1)


def constants():
    c = np.zeros((P, C_END), np.float32)
    c[:, C_ID:C_ID + P] = np.eye(P)
    c[:, C_ONE:C_ONE + P] = 1.0
    half = ROT // 2
    for m in range(half):
        c[m + half, C_ROT + m] = -1.0
        c[m, C_ROT + m + half] = 1.0
    r = np.arange(P)
    later = np.where(r[None, :] <= r[:, None], 0.0, -BIG)
    c[:, C_MASK:C_MASK + P] = later
    c[:, C_MASK + SEQ:C_MASK + 384] = later
    c[:, C_TRIT:C_TRIT + P] = later.T
    pos = np.concatenate([np.arange(SEQ), np.full(NB, PAST)]).astype(np.float32)
    inv = (THETA ** (-(np.arange(half, dtype=np.float64) * 2.0) / ROT)).astype(np.float32)
    ang = (inv[:, None] * pos[None, :]).astype(np.float64)
    c[:, C_COS:C_COS + T] = 1.0
    for s in range(2):
        c[s * half:(s + 1) * half, C_COS:C_COS + T] = np.cos(ang)
        c[s * half:(s + 1) * half, C_SIN:C_SIN + T] = np.sin(ang)
    c[:, C_DEL:C_DEL + 64] = np.eye(NB).reshape(1, 64)
    c[:, C_RANK:C_RANK + 32] = np.repeat(np.arange(NBLK)[::-1], HEADS)[None, :]
    c[:, C_EPS] = EPS
    return c


_INS = ["x_prompt", "x_sample", "cache_k", "cache_v", "page_table", "state_mlstm_C", "state_mlstm_n", "state_mlstm_m",
        "w_in", "w_proj_attn", "w_proj_mlstm", "w_out"]
_OUTS = [("y_p", (1, SEQ, D)), ("y_s", (NB, 1, D)), ("k_p", (SEQ, D)), ("v_p", (SEQ, D)),
         ("C_p", (1, 1, MH, MHD, MHD)), ("n_p", (1, 1, MH, MHD)), ("m_p", (MH, 1)),
         ("k_s", (HEADS * NB, HD)), ("v_s", (HEADS * NB, HD)),
         ("C_s", (1, NB, MH, MHD, MHD)), ("n_s", (1, NB, MH, MHD)), ("m_s", (1, NB, MH))]


def kernel(**inputs):
    import concourse.bacc as _bacc
    from concourse.bass_utils import run_bass_kernel_spmd as _run

    nc = _bacc.Bacc("TRN2", target_bir_lowering=False, num_devices=1, dynamic_dma_scratch_size=4096)
    arrays, a, o = {}, {}, {}
    for name in _INS:
        x = np.ascontiguousarray(inputs[name])
        arrays[f"in_{name}"] = x
        a[name] = nc.dram_tensor(f"in_{name}", x.shape, mybir.dt.from_np(x.dtype), kind="ExternalInput").ap()
    def cols(name):
        return np.ascontiguousarray(inputs[name]).reshape(-1, P).T

    w_in = np.ascontiguousarray(inputs["w_in"])[0]
    laid_out = {
        "consts": constants(),
        "columns": np.concatenate([cols(n) for n in ("norm_w", "q_norm_w", "k_norm_w", "mh_norm_w")], axis=1),
        "gate_bias": np.ascontiguousarray(inputs["b_gates"]).reshape(2, MH).T,
        "gate_weights": w_in[:, GATES:].reshape(KC, P, 2 * MH).transpose(1, 0, 2).reshape(P, KC * 2 * MH),
    }
    for name, x in laid_out.items():
        x = np.ascontiguousarray(x)
        arrays[f"in_{name}"] = x
        a[name] = nc.dram_tensor(f"in_{name}", x.shape, F32, kind="ExternalInput").ap()
    for name, shape in _OUTS:
        o[name] = nc.dram_tensor(f"out_{name}", shape, F32, kind="ExternalOutput").ap()
    build(nc, a, o)
    r = _run(nc, [arrays], core_ids=[0]).results[0]
    g = {name: r[f"out_{name}"] for name, _ in _OUTS}
    rows = (1, 1, SEQ, HEADS, HD)
    by_sample = (lambda x: x.reshape(HEADS, NB, HD).transpose(1, 0, 2).reshape(1, NB, 1, HEADS, HD))
    return (g["y_p"], g["y_s"], g["k_p"].reshape(rows), g["v_p"].reshape(rows), g["C_p"], g["n_p"], g["m_p"].reshape(1, 1, MH),
            by_sample(g["k_s"]), by_sample(g["v_s"]), g["C_s"], g["n_s"], g["m_s"])
```
